# Optimizing a Trainium2 kernel written in Bass

```python
import math
import jax
import jax.numpy as jnp
from jax import lax
import numpy as np

D_MODEL = 1024
BATCH = 1
SEQ = 512
DEPTH = 1

N_HEADS_A = 8
HEAD_DIM = 64
Q_RANK = 256
KV_RANK = 128
N_IDX_HEADS = 8
IDX_DIM = 64
TOPK_MAX = 256
Q_BLOCK = 128
REL_BUCKETS = 32
REL_MAX_DIST = 128
CONV_CH = 256
CONV_WIDTH = 3
N_MEM = 256
N_MEM_HEADS = 4
MIX_A = N_HEADS_A * HEAD_DIM
MIX_C = N_MEM_HEADS * HEAD_DIM
MIX_WIDTH = MIX_A + CONV_CH + MIX_C
IN_SIZES = (Q_RANK, KV_RANK, IDX_DIM, N_IDX_HEADS, CONV_CH, CONV_CH, CONV_CH, MIX_C)
IN_COLS = Q_RANK + KV_RANK + IDX_DIM + N_IDX_HEADS + 3 * CONV_CH + MIX_C
N_EXPERTS = 64
N_GROUPS = 8
TOPK_GROUPS = 4
TOP_K = 8
D_EXPERT = 256
ROUTED_SCALE = 2.5
MOE_BLOCK = 256
ALPHA = (2.0 * DEPTH) ** 0.25
BETA = (8.0 * DEPTH) ** -0.25
LN_EPS = 1e-5
RMS_EPS = 1e-6

kernel_name = 'hybrid_dsa_shortconv_memxattn_moe_deepnorm'

def layer_norm(x, g, b):
    xf = x.astype(jnp.float32)
    mu = jnp.mean(xf, axis=-1, keepdims=True)
    var = jnp.mean(jnp.square(xf - mu), axis=-1, keepdims=True)
    return ((xf - mu) * lax.rsqrt(var + LN_EPS) * g.astype(jnp.float32) + b.astype(jnp.float32)).astype(x.dtype)

def rms_norm(x, g):
    xf = x.astype(jnp.float32)
    return (xf * lax.rsqrt(jnp.mean(jnp.square(xf), axis=-1, keepdims=True) + RMS_EPS) * g.astype(jnp.float32)).astype(x.dtype)

def t5_bucket(rel):
    n = jnp.maximum(rel, 0)
    max_exact = REL_BUCKETS // 2
    nf = jnp.maximum(n.astype(jnp.float32), 1.0)
    large = max_exact + (jnp.log(nf / max_exact) / math.log(REL_MAX_DIST / max_exact) * (REL_BUCKETS - max_exact)).astype(jnp.int32)
    large = jnp.minimum(large, REL_BUCKETS - 1)
    return jnp.where(n < max_exact, n, large)

def swiglu(h, wg, wu, wd):
    return (jax.nn.silu(h @ wg) * (h @ wu)) @ wd

def dsa_attention(c_q, c_kv, k_idx, idx_w, w_uq, w_uk, w_uv, w_qidx, rel_bias):
    B, S, _ = c_q.shape
    k_sel = min(TOPK_MAX, S // 4)
    nb = S // Q_BLOCK
    q = jnp.einsum('bsr,rhd->bshd', c_q, w_uq)
    q_lat = jnp.einsum('bshd,chd->bshc', q, w_uk) * (HEAD_DIM ** -0.5)
    q_idx = jnp.einsum('bsr,rhd->bshd', c_q, w_qidx)
    idx_w = idx_w * (N_IDX_HEADS ** -0.5 * IDX_DIM ** -0.5)
    kpos = jnp.arange(S)

    def blocks(a):
        return a.reshape((B, nb, Q_BLOCK) + a.shape[2:]).swapaxes(0, 1)

    def attend_block(args):
        ql, qi, wi, start = args
        qpos = start + jnp.arange(Q_BLOCK)
        dots = jnp.einsum('bqhd,bsd->bqhs', qi, k_idx).astype(jnp.float32)
        score = jnp.einsum('bqhs,bqh->bqs', jax.nn.relu(dots), wi.astype(jnp.float32))
        score = jnp.where(kpos[None, None, :] <= qpos[None, :, None], score, -jnp.inf)
        _, sel = lax.top_k(score, k_sel)
        kv_sel = jax.vmap(lambda c, i: c[i])(c_kv, sel)
        rel = qpos[None, :, None] - sel
        bias = jnp.moveaxis(rel_bias[t5_bucket(rel)], -1, -2)
        logits = jnp.einsum('bqhc,bqkc->bqhk', ql, kv_sel).astype(jnp.float32) + bias.astype(jnp.float32)
        logits = jnp.where((rel >= 0)[:, :, None, :], logits, -jnp.inf)
        p = jax.nn.softmax(logits, axis=-1).astype(kv_sel.dtype)
        return jnp.einsum('bqhk,bqkc->bqhc', p, kv_sel)

    starts = jnp.arange(nb, dtype=jnp.int32) * Q_BLOCK
    o_lat = lax.map(attend_block, (blocks(q_lat), blocks(q_idx), blocks(idx_w), starts))
    o_lat = o_lat.swapaxes(0, 1).reshape(B, S, N_HEADS_A, KV_RANK)
    o = jnp.einsum('bshc,chd->bshd', o_lat, w_uv)
    return o.reshape(B, S, MIX_A)

def short_conv(b_gate, c_gate, h, conv_w):
    S = h.shape[1]
    u = c_gate * h
    u_pad = jnp.pad(u, ((0, 0), (CONV_WIDTH - 1, 0), (0, 0)))
    y = conv_w[0] * u_pad[:, 0:S]
    for j in range(1, CONV_WIDTH):
        y = y + conv_w[j] * u_pad[:, j:j + S]
    return b_gate * y

def memory_attention(q_in, mem, w_mem_k, w_mem_v):
    B, S, _ = q_in.shape
    q = q_in.reshape(B, S, N_MEM_HEADS, HEAD_DIM)
    k = (mem @ w_mem_k).reshape(B, -1, N_MEM_HEADS, HEAD_DIM)
    v = (mem @ w_mem_v).reshape(B, -1, N_MEM_HEADS, HEAD_DIM)
    logits = jnp.einsum('bshd,bmhd->bhsm', q, k).astype(jnp.float32) * (HEAD_DIM ** -0.5)
    p = jax.nn.softmax(logits, axis=-1).astype(v.dtype)
    return jnp.einsum('bhsm,bmhd->bshd', p, v).reshape(B, S, MIX_C)

def route(xt, w_router, router_bias):
    T = xt.shape[0]
    s = jax.nn.sigmoid(xt.astype(jnp.float32) @ w_router.astype(jnp.float32))
    s_choice = s + router_bias.astype(jnp.float32)
    grp = s_choice.reshape(T, N_GROUPS, N_EXPERTS // N_GROUPS)
    grp_score = jnp.sum(lax.top_k(grp, 2)[0], axis=-1)
    _, gidx = lax.top_k(grp_score, TOPK_GROUPS)
    gmask = jnp.any(gidx[..., None] == jnp.arange(N_GROUPS), axis=-2)
    emask = jnp.repeat(gmask, N_EXPERTS // N_GROUPS, axis=-1)
    _, top_idx = lax.top_k(jnp.where(emask, s_choice, -jnp.inf), TOP_K)
    top_s = jnp.take_along_axis(s, top_idx, axis=-1)
    top_w = top_s / jnp.sum(top_s, axis=-1, keepdims=True) * ROUTED_SCALE
    return top_idx, top_w

def routed_experts(xt, top_idx, top_w, w_gate, w_up, w_down):
    T, D = xt.shape
    n_slots = T * TOP_K
    flat_e = top_idx.reshape(-1)
    order = jnp.argsort(flat_e)
    sorted_e = flat_e[order]
    counts = jnp.bincount(flat_e, length=N_EXPERTS)
    padded = (counts + MOE_BLOCK - 1) // MOE_BLOCK * MOE_BLOCK
    pad_end = jnp.cumsum(padded)
    pad_start = pad_end - padded
    grp_start = jnp.cumsum(counts) - counts
    dest = pad_start[sorted_e] + (jnp.arange(n_slots) - grp_start[sorted_e])
    n_blocks = -(-n_slots // MOE_BLOCK) + N_EXPERTS
    n_rows = n_blocks * MOE_BLOCK
    row_tok = jnp.full((n_rows,), T, jnp.int32).at[dest].set((order // TOP_K).astype(jnp.int32))
    row_w = jnp.zeros((n_rows,), xt.dtype).at[dest].set(top_w.reshape(-1)[order])
    block_e = jnp.minimum(jnp.searchsorted(pad_end, jnp.arange(n_blocks) * MOE_BLOCK, side='right'), N_EXPERTS - 1)
    xt_pad = jnp.concatenate([xt, jnp.zeros((1, D), xt.dtype)], axis=0)

    def expert_block(acc, blk):
        tok, wt, e = blk
        y = swiglu(xt_pad[tok], w_gate[e], w_up[e], w_down[e]) * wt[:, None]
        return acc.at[tok].add(y), None

    acc, _ = lax.scan(expert_block, jnp.zeros((T + 1, D), xt.dtype),
                      (row_tok.reshape(n_blocks, MOE_BLOCK), row_w.reshape(n_blocks, MOE_BLOCK), block_e))
    return acc[:T]

def moe_ffn(x, w_router, router_bias, w_e_gate, w_e_up, w_e_down, w_s_gate, w_s_up, w_s_down):
    B, S, D = x.shape
    xt = x.reshape(B * S, D)
    top_idx, top_w = route(xt, w_router, router_bias)
    routed = routed_experts(xt, top_idx, top_w.astype(xt.dtype), w_e_gate, w_e_up, w_e_down)
    shared = swiglu(xt, w_s_gate, w_s_up, w_s_down)
    return (routed + shared).reshape(B, S, D)

def hybrid_layer(x, mem, w_in, q_norm_g, kv_norm_g, w_uq, w_uk, w_uv, w_qidx, rel_bias, conv_w,
                 w_mem_k, w_mem_v, w_out, ln1_g, ln1_b, w_router, router_bias, w_e_gate, w_e_up,
                 w_e_down, w_s_gate, w_s_up, w_s_down, ln2_g, ln2_b):
    proj = x @ w_in
    c_q, c_kv, k_idx, idx_w, g_b, g_c, h_conv, q_mem = jnp.split(proj, np.cumsum(IN_SIZES)[:-1], axis=-1)
    c_q = rms_norm(c_q, q_norm_g)
    c_kv = rms_norm(c_kv, kv_norm_g)
    y_a = dsa_attention(c_q, c_kv, k_idx, idx_w, w_uq, w_uk, w_uv, w_qidx, rel_bias)
    y_b = short_conv(g_b, g_c, h_conv, conv_w)
    y_c = memory_attention(q_mem, mem, w_mem_k, w_mem_v)
    mix = jnp.concatenate([y_a, y_b, y_c], axis=-1) @ w_out
    x = layer_norm(ALPHA * x + mix, ln1_g, ln1_b)
    ffn = moe_ffn(x, w_router, router_bias, w_e_gate, w_e_up, w_e_down, w_s_gate, w_s_up, w_s_down)
    return layer_norm(ALPHA * x + ffn, ln2_g, ln2_b)

def setup_inputs(seed: int = 0) -> dict:
    key = jax.random.key(seed)
    ks = iter(jax.random.split(key, 32))
    L = DEPTH

    def nrm(shape, fan_in, scale=1.0):
        return jax.random.normal(next(ks), shape, jnp.float32) * (scale * fan_in ** -0.5)

    def gain(shape):
        return 1.0 + 0.05 * jax.random.normal(next(ks), shape, jnp.float32)

    def small(shape, s):
        return s * jax.random.normal(next(ks), shape, jnp.float32)

    return {
        'x': jax.random.normal(next(ks), (BATCH, SEQ, D_MODEL), jnp.float32),
        'mem': jax.random.normal(next(ks), (BATCH, N_MEM, D_MODEL), jnp.float32),
        'w_in': nrm((L, D_MODEL, IN_COLS), D_MODEL),
        'q_norm_g': gain((L, Q_RANK)),
        'kv_norm_g': gain((L, KV_RANK)),
        'w_uq': nrm((L, Q_RANK, N_HEADS_A, HEAD_DIM), Q_RANK),
        'w_uk': nrm((L, KV_RANK, N_HEADS_A, HEAD_DIM), KV_RANK),
        'w_uv': nrm((L, KV_RANK, N_HEADS_A, HEAD_DIM), KV_RANK, BETA),
        'w_qidx': nrm((L, Q_RANK, N_IDX_HEADS, IDX_DIM), Q_RANK),
        'rel_bias': small((REL_BUCKETS, N_HEADS_A), 0.5),
        'conv_w': nrm((L, CONV_WIDTH, CONV_CH), CONV_WIDTH),
        'w_mem_k': nrm((L, D_MODEL, MIX_C), D_MODEL),
        'w_mem_v': nrm((L, D_MODEL, MIX_C), D_MODEL, BETA),
        'w_out': nrm((L, MIX_WIDTH, D_MODEL), MIX_WIDTH, BETA),
        'ln1_g': gain((L, D_MODEL)),
        'ln1_b': small((L, D_MODEL), 0.02),
        'w_router': nrm((L, D_MODEL, N_EXPERTS), D_MODEL),
        'router_bias': small((L, N_EXPERTS), 0.01),
        'w_e_gate': nrm((L, N_EXPERTS, D_MODEL, D_EXPERT), D_MODEL),
        'w_e_up': nrm((L, N_EXPERTS, D_MODEL, D_EXPERT), D_MODEL),
        'w_e_down': nrm((L, N_EXPERTS, D_EXPERT, D_MODEL), D_EXPERT, BETA),
        'w_s_gate': nrm((L, D_MODEL, D_EXPERT), D_MODEL),
        'w_s_up': nrm((L, D_MODEL, D_EXPERT), D_MODEL),
        'w_s_down': nrm((L, D_EXPERT, D_MODEL), D_EXPERT, BETA),
        'ln2_g': gain((L, D_MODEL)),
        'ln2_b': small((L, D_MODEL), 0.02),
    }

def reference(x, mem, w_in, q_norm_g, kv_norm_g, w_uq, w_uk, w_uv, w_qidx, rel_bias, conv_w,
              w_mem_k, w_mem_v, w_out, ln1_g, ln1_b, w_router, router_bias, w_e_gate, w_e_up,
              w_e_down, w_s_gate, w_s_up, w_s_down, ln2_g, ln2_b):
    for l in range(DEPTH):
        x = hybrid_layer(x, mem, w_in[l], q_norm_g[l], kv_norm_g[l], w_uq[l], w_uk[l], w_uv[l], w_qidx[l],
                         rel_bias, conv_w[l], w_mem_k[l], w_mem_v[l], w_out[l], ln1_g[l], ln1_b[l],
                         w_router[l], router_bias[l], w_e_gate[l], w_e_up[l], w_e_down[l],
                         w_s_gate[l], w_s_up[l], w_s_down[l], ln2_g[l], ln2_b[l])
    return x


_drawn_inputs = setup_inputs


def setup_inputs(seed=0):
    import zlib

    import numpy as np

    out = dict(_drawn_inputs(seed))
    spreads = {}
    factors = {'kv_norm_g': 3.637, 'ln2_b': 2.812}
    for name, (base, spread) in spreads.items():
        noise = np.random.default_rng([zlib.crc32(name.encode()), seed]).standard_normal(out[name].shape)
        drawn = base * np.exp(spread * noise) if base else spread * noise
        out[name] = jnp.asarray(drawn.astype(out[name].dtype))
    for name, factor in factors.items():
        out[name] = (out[name] * factor).astype(out[name].dtype)
    return out
```

```python
import math
from contextlib import ExitStack

import concourse.bass as bass
import numpy as np
from concourse import mybir

F32 = mybir.dt.float32
U32 = mybir.dt.uint32
I32 = mybir.dt.int32
ALU = mybir.AluOpType
ACT = mybir.ActivationFunctionType
AX = mybir.AxisListType

P = 128
T, D = 512, 1024
TB = T // P
DK = D // P
M = 256
MB = M // P
QR, KVR, IDX, NI = 256, 128, 64, 8
H, HD = 8, 64
CC = 256
MH = 4
TOKEN_COLS = QR + KVR + IDX + NI
IN_COLS = TOKEN_COLS + 3 * CC + MH * HD
TOPK = min(256, T // 4)
BUCKETS, MAX_DIST = 32, 128
E, G, TOPG, TOPE = 64, 8, 4, 8
EG = E // G
FE = 256
CAP = 128
ROUNDS = T // CAP
SLOTS = 4
AHEAD = 4
UNROLL = 8
SKEW = 640
ALPHA = 2.0 ** 0.25
LN_EPS, RMS_EPS = 1e-5, 1e-6
NEG = -3.0e38
TAKEN = -3.3e38
MIDWAY = -3.2e38
FAR = float(1 << 20)
KB = 1024
BASE = 16512

RING = 4
QBS = (3, 2, 1)
FILLS_S = (
    [("xT", b, 0) for b in range(TB)] + [("memT", b, 0) for b in range(MB)]
    + [("kmT", m) for m in range(2)]
    + [("ukT",)] + [("cT", b) for b in range(TB)] + [("qiT", m) for m in range(4)]
    + [("dot", q, h) for q in QBS for h in range(NI)]
    + [("vm", b) for b in range(MB)] + [("qT", m) for m in range(4)] + [("qm", m) for m in range(2)]
    + [("ml", b, j) for b in range(TB) for j in range(2)]
    + [(k, c) for c in range(2) for k in ("gc", "gb")]
    + [("ql", h) for h in range(H)]
    + [("pmT", b, m) for b in range(TB) for m in range(MB)] + [("yc", j) for j in range(2)]
    + [f for q in range(TB) for g in range(2) for f in [("pT", q, g, s) for s in range(q + 1)] + [("ol", q, g)]]
    + [("ya", m) for m in range(4)]
    + [f for b in range(TB) for f in (("x1T", b, 0), ("rt", b))]
    + [("shT", b) for b in range(TB)]
)
FILLS_V = (
    [("bias", n) for n in range(2)]
    + [("xT", b, 1) for b in range(TB)] + [("memT", b, 1) for b in range(MB)]
    + [("proj", b) for b in range(TB)]
    + [("hc", c) for c in range(2)]
    + [("lg", q, g, h) for q in range(TB) for g in range(2) for h in range(4)]
    + [("mo", 0, 0), ("mo", 0, 1)] + [f for b in range(1, TB) for f in (("mo", b, 0), ("x1T", b - 1, 1), ("mo", b, 1))]
    + [("gu", 0), ("x1T", 3, 1), ("gu", 1)]
    + [("yd", 0, 0), ("yd", 0, 1), ("pos",), ("cnt",), ("gu", 2), ("slots",), ("gu", 3)]
    + [("yd", b, j) for b in range(1, TB) for j in range(2)]
)
NO_S = {f: n for n, f in enumerate(FILLS_S)}
NO_V = {f: n for n, f in enumerate(FILLS_V)}


def bucket_table():
    n = np.arange(T)
    exact = BUCKETS // 2
    far = np.log(np.maximum(n, 1).astype(np.float32) / np.float32(exact)) / np.float32(math.log(MAX_DIST / exact))
    bucket = np.where(n < exact, n, np.minimum(exact + (far * np.float32(BUCKETS - exact)).astype(np.int32), BUCKETS - 1))
    table = np.zeros((BUCKETS, SKEW), np.float32)
    table[bucket, n + P - 1] = 1.0
    return table


def layer_kernel(nc, a, out):
    with ExitStack() as ctx:
        build(nc, ctx, a, out)


def build(nc, ctx, a, out):
    def at(name, kb, *shape, dt=F32):
        return nc.alloc_sbuf_tensor_at(name, [P, *shape], dt, offset=BASE + int(kb * KB))

    def sem(name):
        return ctx.enter_context(nc.semaphore(name))

    def dram(name, *shape):
        return nc.dram_tensor(name, shape, F32, kind="Internal").ap()

    w_in = at("w_in", 0, DK, IN_COLS)
    w_out = at("w_out_sb", 0, DK, D)
    g1 = at("g1", 32, D)
    b1 = at("b1", 36, D)
    w_rt = at("w_rt", 40, DK, E)
    xT = at("xT", 48, DK, T)
    qlT = at("qlT", 48, H, T)
    mem_sb = at("mem_sb", 64, MB, D)
    memT = at("memT", 72, DK, M)
    wmk = at("wmk", 80, DK, MH * HD)
    wmv = at("wmv", 88, DK, MH * HD)
    lm = at("lm", 64, TB, MH, M)
    pmT = at("pmT", 80, MB, MH, T)
    olT = at("olT", 64, H, T)
    X = at("X", 96, TB, D)
    w_uq = at("w_uq_sb", 112, 2, H * HD)
    w_qi = at("w_qi", 116, 2, NI * IDX)
    relu = at("relu", 120, 4, T)
    mixT = at("mixT", 112, DK, T)
    x1T = at("x1T", 128, DK, T)
    B = at("B", 128, H, T)
    sh_acc = at("sh_acc", 112, TB, D)
    qT = at("qT", 144, 4, T)
    qiT = at("qiT", 152, 4, T)
    qmT = at("qmT", 152, 2, T)
    lg = at("lg", 144, 2, 4, T)
    sel = at("sel", 160, 3, T)
    sh_w = at("sh_w", 144, 24 * KB // 4)
    proj = at("proj", 166, TB, QR + KVR)
    kk = at("kk", 172, TB, 2, IDX)
    gcT = at("gcT", 166, 2, T)
    gbT = at("gbT", 170, 2, T)
    u = at("u", 174, 2, T + 2)
    cv = at("cv", 178.125, 2, T)
    pT = at("pT", 168, 4, T)
    latT = at("latT", 182.5, 4, T)
    ckvn = at("ckvn", 190.5, TB, KVR)
    w_uk = at("w_uk_sb", 192.5, H * HD)
    w_uv = at("w_uv_sb", 194.5, H * HD)
    ukT = at("ukT", 196.5, 4, P)
    kmT = at("kmT", 198.5, 2, M)
    vm = at("vm", 200.5, MB, MH * HD)
    onehot = at("onehot", 200.5, SKEW)
    gq = at("gq", 196.5, QR)
    gkv = at("gkv", 197.5, KVR)
    rel = at("rel", 198, H)
    square = at("square", 178.5, QR)
    rv = at("rv", 178.5, SKEW)
    ident = at("ident", 203, P)
    causal = at("causal", 203.5, P)
    small = 204.0
    ss = at("ss", small, 2, TB)
    rms = at("rms", small + .03125, 2, TB)
    iw = at("iw", small + .0625, TB, NI)
    top8 = at("top8", small + .875, 3, 8)
    cw = at("cw", small + .21875, 2, 3)
    mmax = at("mmax", small + .25, TB, MH)
    msum = at("msum", small + .3125, TB, MH)
    amax = at("amax", small + .375, 2 * TB, 4)
    asum = at("asum", small + .5, 2 * TB, 4)
    bn = at("bn", small + .625, TB, 2, 6)
    mv = at("mv", small + .8125, TB, 2)
    rstd = at("rstd", small + .84375, TB)
    zeros = at("zeros", 205, 256)
    W = [at(f"W{s}", 24 * s, 24 * KB // 4) for s in range(SLOTS)]
    xg = [at(f"xg{i}", kb, D) for i, kb in enumerate((128, 132, 160, 164))]
    xgT = [at(f"xgT{i}", 136 + 4 * i, DK, CAP) for i in range(2)]
    y = [at(f"y{i}", 144 + 4 * i, D) for i in range(2)]
    oh = [at(f"oh{i}", 182.5 + 2 * i, TB, CAP) for i in range(AHEAD)]
    h_sb = at("h_sb", 156, FE)
    sg = at("sg", 157, FE)
    hT = at("hT", 158, 2, CAP)
    sh_sg = at("sh_sg", 168, FE)
    sh_h = at("sh_h", 196.5, TB, FE)
    sh_hT = at("sh_hT", 200.5, 2, 2, P)
    sg_r = at("sg_r", 171, TB, E)
    sc = at("sc", 172, TB, E)
    rb = at("rb", 173, E)
    g8 = at("g8", 173.25, TB, G, 8)
    gs = at("gs", 174.25, TB, G)
    gtop = at("gtop", 174.375, TB, 8)
    gidx = at("gidx", 174.5, TB, 8, dt=U32)
    gif = at("gif", 174.625, TB, 8)
    gcmp = at("gcmp", 175, TB, G, TOPG)
    gmask = at("gmask", 175.5, TB, G)
    etop = at("etop", 175.625, TB, 8)
    cand = at("cand", 176, TB, E)
    taken = at("taken", 177, TB, E)
    wts = at("wts", 178, TB, E)
    wsum = at("wsum", 179, TB)
    wrec = at("wrec", 179.03125, TB)
    posm = at("posm", 179.5, TB, E)
    tri = at("tri", 190.5, P)
    ones = at("ones", 191, P)
    iota_c = at("iota_c", 191.5, CAP)
    tok = at("tok", 192, TB)
    giota = at("giota", 192.0625, G)
    cnt = at("cnt", 192.125, 1)
    cnt_i = at("cnt_i", 192.15625, 1, dt=I32)
    idx_u = at("idx_u", 181.75, UNROLL, dt=U32)
    w_slot = at("w_slot", 182, UNROLL)
    tab = at("tab", 192.5, TB, E, 2)
    yr = at("yr", 0, TB, 2, D)
    g2 = at("g2", 168, D)
    b2 = at("b2", 152, D)
    bn2 = at("bn2", 173.5, TB, 2, 6)
    mv2 = at("mv2", 173.75, TB, 2)
    rstd2 = at("rstd2", 173.875, TB)

    bias_dram = dram("bias_rows", H, SKEW)
    x1_dram = dram("x1_rows", T, D)
    y_dram = [dram(f"y_rows{i}", T, D) for i in range(2)]

    bank = [ctx.enter_context(nc.psum_tensor(f"bank{i}", [P, 512], F32)) for i in range(8)]

    s_filled, s_emptied = sem("s_filled"), sem("s_emptied")
    v_filled, v_emptied = sem("v_filled"), sem("v_emptied")
    loaded = {n: sem(f"loaded_{n}") for n in (
        "x0", "x1", "x2", "x3", "w_tok", "w_chan", "mem", "wmk", "wmv", "uq", "qi", "uk", "uv", "bucket",
        "rel", "gq", "gkv", "cw", "bias", "w_out", "g1", "b1", "rt", "rb", "sh", "g2", "b2")}
    y_cleared = sem("y_cleared")
    bias_stored, x1_stored = sem("bias_stored"), sem("x1_stored")
    constants = sem("constants")
    squares = sem("squares")
    normed = sem("normed")
    scored = sem("scored")
    chosen = sem("chosen")
    mem_soft = sem("mem_soft")
    mem_exp = sem("mem_exp")
    conv = sem("conv")
    soft = sem("soft")
    att_exp = sem("att_exp")
    ln1 = sem("ln1")
    root1 = sem("root1")
    routed = sem("routed")
    tables = sem("tables")
    sh_silu = sem("sh_silu")

    w_loaded = [sem(f"w_loaded{s}") for s in range(SLOTS)]
    oh_made = sem("oh_made")
    idx_summed = sem("idx_summed")
    idx_made = sem("idx_made")
    pool_turns = sem("pool_turns")
    xg_clear = sem("xg_clear")
    gathered = [sem(f"gathered{i}") for i in range(4)]
    scattered = [sem(f"scattered{i}") for i in range(2)]
    xgT_summed = sem("xgT_summed")
    xgT_s, xgT_v = sem("xgT_s"), sem("xgT_v")
    gu_summed = sem("gu_summed")
    silu_made = sem("silu_made")
    h_made = sem("h_made")
    hT_summed = sem("hT_summed")
    hT_made = sem("hT_made")
    down_summed = sem("down_summed")
    y_s, y_v = sem("y_s"), sem("y_v")
    over = {n: sem(f"over_{n}") for n in (
        "shift", "w", "oh", "idxp", "idx", "gat", "xgTp", "xgTs", "xgTv", "gu", "silu", "h", "hTp", "hT", "dn", "ys", "yv", "sc")}
    rows_loaded = [sem(f"rows_loaded{b}") for b in range(TB)]
    summed = sem("summed")
    root2 = sem("root2")
    stored = sem("stored")

    def fill_s(pe, f):
        n = NO_S[f]
        if n >= RING:
            pe.wait_ge(s_emptied, n - RING + 1)
        return bank[n % RING]

    def fill_v(pe, f):
        n = NO_V[f]
        if n >= RING:
            pe.wait_ge(v_emptied, n - RING + 1)
        return bank[RING + n % RING]

    def full_s(act, f):
        act.wait_ge(s_filled, NO_S[f] + 1)
        return bank[NO_S[f] % RING]

    def full_v(dve, f):
        dve.wait_ge(v_filled, NO_V[f] + 1)
        return bank[RING + NO_V[f] % RING]

    def emptied_s(eng, f):
        eng.wait_ge(s_emptied, NO_S[f] + 1)

    def emptied_v(eng, f):
        eng.wait_ge(v_emptied, NO_V[f] + 1)

    def wait_dma(eng, name, n=1):
        eng.wait_ge(loaded[name], 16 * n)

    NORMED = 2 + 1 + 2 * TB
    def scores_until(q, h):
        return QBS.index(q) * (NI + 1) + h + 1
    def chosen_after(r, phase, n):
        return (2 * r + phase) * len(QBS) + n + 1
    CONV = 4
    UNIT = 4 + 1 + 1 + 4
    units = [(q, g) for q in range(TB) for g in range(2)]

    def att_steps(i, n):
        if n <= 5:
            return 5 * (i + 1) + (UNIT - 5) * max(i - 1, 0) - 5 + n
        return 5 * min(i + 2, len(units)) + (UNIT - 5) * i + n - 5

    LN = 2 + 1 + 1 + 1 + 3
    def weights(slot):
        return slot[:, 0:4096].rearrange("p (g k f) -> p g k f", g=2, k=DK), slot[:, 4096:6144].rearrange("p (k n) -> p k n", k=2)
    sh_gu, sh_d = weights(sh_w)
    Wgu, Wd = zip(*[weights(w) for w in W])
    w_rows = lambda ap: ap.rearrange("(p k) n -> p k n", p=P)

    FINAL = 2 + LN

    TAKEN_STEP = 1 + G + 1 + 1 + 1 + 1 + 1 + 1 + 1 + 1 + 1 + 1 + 1 + 1
    ROUTE = TAKEN_STEP + 5

    def slots4(b):
        return b[:, :].rearrange("p (k c) -> p k c", k=4)[:, :, 0:CAP]

    def slot_weight(buf):
        return w_slot[0:CAP, buf:buf + 1]

    def y_free(e, n):
        return (e - (n % 2)) * 8

    def run_experts(eng, step):
        for e in range(AHEAD):
            step(e, e, first=e == 0)
        with eng.Fori(0, (E - 2 * AHEAD) // UNROLL) as i:
            for n in range(AHEAD, AHEAD + UNROLL):
                step(i * UNROLL + n, n)
        for e in range(E - AHEAD, E):
            step(e, e % UNROLL, last=e == E - 1)

    block = ctx.enter_context(nc.Block())

    @block.sync
    def _(sp):
        x_rows = a["x"][0].rearrange("(b p) d -> p b d", p=P)
        win = w_rows(a["w_in"][0])
        for b in range(TB):
            sp.dma_start(X[:, b, :], x_rows[:, b, :]).then_inc(loaded[f"x{b}"], 16)
        sp.dma_start(w_in[:, :, 0:TOKEN_COLS], win[:, :, 0:TOKEN_COLS]).then_inc(loaded["w_tok"], 16)
        sp.dma_start(mem_sb[:, :, :], a["mem"][0].rearrange("(b p) d -> p b d", p=P)).then_inc(loaded["mem"], 16)
        sp.dma_start(wmk[:, :, :], w_rows(a["w_mem_k"][0])).then_inc(loaded["wmk"], 16)
        sp.dma_start(wmv[:, :, :], w_rows(a["w_mem_v"][0])).then_inc(loaded["wmv"], 16)
        sp.dma_start(w_in[:, :, TOKEN_COLS:], win[:, :, TOKEN_COLS:]).then_inc(loaded["w_chan"], 16)
        sp.wait_ge(s_filled, NO_S["gb", 1] + 1)
        sp.dma_start(w_out[:, :, :], a["w_out"][0].rearrange("(k p) n -> p k n", p=P)).then_inc(loaded["w_out"], 16)
        for name, dst, src in (("g1", g1, a["ln1_g"]), ("b1", b1, a["ln1_b"])):
            sp.dma_start(dst[:, :], src[0].partition_broadcast(P)).then_inc(loaded[name], 16)
        sp.dma_start(w_rt[:, :, :], w_rows(a["w_router"][0])).then_inc(loaded["rt"], 16)
        sp.wait_ge(s_filled, NO_S["ol", TB - 1, 1] + 1)
        sp.dma_start(sh_gu[:, 0, :, :], w_rows(a["w_s_gate"][0])).then_inc(loaded["sh"], 16)
        sp.dma_start(sh_gu[:, 1, :, :], w_rows(a["w_s_up"][0])).then_inc(loaded["sh"], 16)
        sp.dma_start(sh_d, w_rows(a["w_s_down"][0])).then_inc(loaded["sh"], 16)
        sp.dma_start(rb[:, :], a["router_bias"][0].partition_broadcast(P)).then_inc(loaded["rb"], 16)

        def row(t, e):
            return t[0][bass.ds(e, 1)].rearrange("e r n -> (e r) n")

        def load_e(e, s, done):
            sp.dma_start(Wgu[s][:, 0, :, :], w_rows(row(a["w_e_gate"], e))).then_inc(done, 16)
            sp.dma_start(Wgu[s][:, 1, :, :], w_rows(row(a["w_e_up"], e))).then_inc(done, 16)
            sp.dma_start(Wd[s], w_rows(row(a["w_e_down"], e))).then_inc(done, 16)

        sp.wait_ge(s_filled, NO_S["ya", 3] + 1)
        load_e(0, 2, w_loaded[2])
        load_e(1, 3, w_loaded[3])
        x1_rows = x1_dram.rearrange("(b p) d -> p b d", p=P)
        for b in range(TB):
            sp.wait_ge(ln1, LN * (b + 1))
            sp.dma_start(x1_rows[:, b, :], X[:, b, :]).then_inc(x1_stored, 16)
        sp.wait_ge(s_filled, NO_S["rt", TB - 1] + 1)
        load_e(2, 0, w_loaded[0])
        load_e(3, 1, w_loaded[1])
        sp.wait_ge(v_filled, NO_V["yd", TB - 1, 1] + 1)
        for name, dst, src in (("g2", g2, a["ln2_g"]), ("b2", b2, a["ln2_b"])):
            sp.dma_start(dst[:, :], src[0].partition_broadcast(P)).then_inc(loaded[name], 16)
        with sp.Fori(1, E // SLOTS) as i:
            for n in range(SLOTS):
                sp.wait_ge(down_summed, (i * SLOTS + (n + 1 - SLOTS)) * 2)
                load_e(i * SLOTS + n, (n + 2) % SLOTS, w_loaded[(n + 2) % SLOTS])
        for i in range(2):
            sp.wait_ge(scattered[i], 16 * (E // 2))
        sp.wait_ge(over["shift"], 1)
        most = sp.value_load(cnt_i[0:1, 0:1], min_val=0, max_val=T)
        with sp.If(most > CAP):
            with sp.Fori(1, ROUNDS) as r:
                with sp.Fori(0, E) as e:
                    n = (r - 1) * E + e
                    sp.wait_ge(over["oh"], n + 1)
                    load_e(e, 0, over["w"])
            sp.wait_ge(over["sc"], 16 * (ROUNDS - 1) * E)
        for b in range(TB):
            for i in range(2):
                sp.dma_start(yr[:, b, i, :], y_dram[i][b * P:(b + 1) * P, :]).then_inc(rows_loaded[b], 16)
        out_rows = out[0].rearrange("(b p) d -> p b d", p=P)
        for b in range(TB):
            sp.wait_ge(summed, FINAL * (b + 1))
            sp.dma_start(out_rows[:, b, :], sh_acc[:, b, :]).then_inc(stored, 16)
        sp.wait_ge(stored, 16 * TB)

    @block.gpsimd
    def _(pool):
        pool.memset(ident[:, :], 0.0).then_inc(constants, 1)
        pool.memset(causal[:, :], 0.0).then_inc(constants, 1)
        pool.wait_ge(constants, 2)
        pool.affine_select(out=ident[:, :], in_=ident[:, :], compare_op=ALU.not_equal, fill=1.0,
                           base=0, pattern=[[-1, P]], channel_multiplier=1).then_inc(constants, 1)
        pool.affine_select(out=causal[:, :], in_=causal[:, :], compare_op=ALU.is_ge, fill=NEG,
                           base=0, pattern=[[-1, P]], channel_multiplier=1).then_inc(constants, 1)
        emptied_v(pool, ("bias", 1))
        pool.dma_start(bias_dram, rv[0:H, :]).then_inc(bias_stored, 16)
        pool.wait_ge(bias_stored, 16)
        skewed = bass.AP(bias_dram.tensor, 0, [[1, P], [SKEW, H], [1, T]])
        pool.dma_start(B[:, :, :], skewed).then_inc(loaded["bias"], 16)
        pool.memset(zeros[:, :], 0.0).then_inc(constants, 1)
        pool.wait_ge(constants, 5)
        for i in range(2):
            for b in range(TB):
                pool.dma_start(y_dram[i][b * P:(b + 1) * P, :].rearrange("p (j c) -> p j c", j=4),
                               zeros[:, :].unsqueeze(1).to_broadcast([P, 4, 256])).then_inc(y_cleared, 16)
        pool.wait_ge(s_filled, NO_S["ol", TB - 1, 1] + 1)
        pool.memset(ones[:, :], 1.0).then_inc(tables, 1)
        pool.memset(tri[:, :], 1.0).then_inc(tables, 1)
        pool.wait_ge(tables, 2)
        pool.affine_select(out=tri[:, :], in_=tri[:, :], compare_op=ALU.is_gt, fill=0.0,
                           base=0, pattern=[[1, P]], channel_multiplier=-1).then_inc(tables, 1)
        pool.iota(iota_c[:, :], [[1, CAP]], base=0, channel_multiplier=0, allow_small_or_imprecise_dtypes=True).then_inc(tables, 1)
        pool.iota(tok[:, :], [[P, TB]], base=0, channel_multiplier=1, allow_small_or_imprecise_dtypes=True).then_inc(tables, 1)
        pool.iota(giota[:, :], [[1, G]], base=0, channel_multiplier=0, allow_small_or_imprecise_dtypes=True).then_inc(tables, 1)
        pool.wait_ge(v_filled, NO_V["gu", TB - 1] + 1)
        for i in range(2):
            pool.memset(xg[i][:, :], 0.0).then_inc(xg_clear, 1)
        pool.wait_ge(xg_clear, 2)
        pool.wait_ge(x1_stored, 16 * TB)

        last_token = pool.to_reg(T - 1)

        def gather(buf, ibuf, done):
            pool.sem_inc(pool_turns, 1)
            pool.indirect_dma_start(out=xg[buf][0:CAP, :], out_offset=None, in_=x1_dram[:, :],
                                    in_offset=bass.IndirectOffsetOnAxis(ap=idx_u[0:CAP, ibuf:ibuf + 1], axis=0),
                                    bounds_check=last_token, oob_is_err=False).then_inc(done, 16)

        def scatter(buf, ibuf, done):
            pool.sem_inc(pool_turns, 1)
            pool.indirect_dma_start(out=y_dram[buf][:, :], out_offset=bass.IndirectOffsetOnAxis(ap=idx_u[0:CAP, ibuf:ibuf + 1], axis=0),
                                    in_=y[buf][0:CAP, :], in_offset=None, bounds_check=last_token, oob_is_err=False,
                                    compute_op=ALU.add).then_inc(done, 16)

        def gather_e(e, n):
            if isinstance(e, int) and e < AHEAD:
                emptied_v(pool, ("slots",))
            else:
                pool.wait_ge(idx_made, (e - AHEAD + 1) * 2)
                pool.wait_ge(xgT_summed, e * 2 - 6)
            gather(n % 4, n % UNROLL, gathered[n % 4])

        def scatter_e(e, n, first=False):
            pool.wait_ge(y_s, e + 1)
            pool.wait_ge(y_v, e + 1)
            if not first:
                pool.wait_ge(scattered[n % 2], y_free(e, n))
            scatter(n % 2, n % UNROLL, scattered[n % 2])

        pool.wait_ge(y_cleared, 2 * TB * 16)
        for e in range(AHEAD):
            if e == 2:
                pool.wait_ge(v_filled, NO_V["yd", TB - 1, 1] + 1)
                for i in (2, 3):
                    pool.memset(xg[i][:, :], 0.0).then_inc(xg_clear, 1)
                pool.wait_ge(xg_clear, 4)
            gather_e(e, e)
        for e in range(AHEAD):
            gather_e(e + AHEAD, e + AHEAD)
            scatter_e(e, e, first=e < 2)
        with pool.Fori(0, (E - 2 * AHEAD) // UNROLL) as i:
            for n in range(AHEAD, AHEAD + UNROLL):
                gather_e(i * UNROLL + (n + AHEAD), n + AHEAD)
                scatter_e(i * UNROLL + n, n)
        for e in range(E - AHEAD, E):
            scatter_e(e, e)
        for i in range(2):
            pool.wait_ge(scattered[i], 16 * (E // 2))
        pool.wait_ge(over["shift"], 1)
        most = pool.value_load(cnt_i[0:1, 0:1], min_val=0, max_val=T)
        with pool.If(most > CAP):
            with pool.Fori(0, (ROUNDS - 1) * E) as n:
                pool.wait_ge(over["idx"], n * 2 + 2)
                gather(0, 0, over["gat"])
                pool.wait_ge(over["ys"], n + 1)
                pool.wait_ge(over["yv"], n + 1)
                scatter(0, 0, over["sc"])
                pool.wait_ge(over["sc"], n * 16 + 16)

    @block.scalar
    def _(act):
        def load(dst, src, name):
            act.dma_start(dst, src).then_inc(loaded[name], 16)

        load(onehot[0:BUCKETS, :], a["buckets"], "bucket")
        load(rel[0:BUCKETS, :], a["rel_bias"], "rel")
        load(w_uk[:, :], a["w_uk"][0].rearrange("c h d -> c (h d)"), "uk")
        load(gq[:, :], a["q_norm_g"][0].partition_broadcast(P), "gq")
        load(gkv[:, :], a["kv_norm_g"][0].partition_broadcast(P), "gkv")
        load(w_qi[:, :, :], a["w_qidx"][0].rearrange("(k p) h d -> p k (h d)", p=P), "qi")
        load(w_uq[:, :, :], a["w_uq"][0].rearrange("(k p) h d -> p k (h d)", p=P), "uq")
        load(w_uv[:, :], a["w_uv"][0].rearrange("c h d -> c (h d)"), "uv")
        for c in range(2):
            for j in range(3):
                load(cw[:, c, j:j + 1], a["conv_w"][0][j:j + 1, c * P:(c + 1) * P].rearrange("o p -> p o"), "cw")

        def empty(f, dst, scale=1.0, view=None):
            b = full_s(act, f)
            act.activation(dst, view(b) if view else b[:, :], ACT.Copy, scale=scale).then_inc(s_emptied, 1)

        four = lambda b: b[:, :].rearrange("p (k t) -> p k t", k=4)
        for b in range(TB):
            empty(("xT", b, 0), xT[:, 0:4, b * P:(b + 1) * P], view=four)
        for b in range(MB):
            empty(("memT", b, 0), memT[:, 0:4, b * P:(b + 1) * P], view=four)
        for b in range(TB):
            emptied_v(act, ("proj", b))
            for k, (lo, n) in enumerate(((0, QR), (QR, KVR))):
                if b or k:
                    act.wait_ge(squares, 2 * b + k)
                else:
                    emptied_v(act, ("proj", 0))
                    act.wait_ge(bias_stored, 16)
                act.activation(square[:, 0:n], proj[:, b, lo:lo + n], ACT.Square,
                               accum_out=ss[:, k, b:b + 1]).then_inc(squares, 1)
        act.wait_ge(normed, 2)
        act.activation(rms[:, :, :], rms[:, :, :], ACT.Sqrt).then_inc(squares, 1)
        for m in range(2):
            empty(("kmT", m), kmT[:, m, :], view=lambda b: b[:, 0:M])
        act.wait_ge(normed, NORMED)
        empty(("ukT",), ukT[:, :, :], view=four)
        for b in range(TB):
            empty(("cT", b), latT[:, :, b * P:(b + 1) * P], view=four)
        for m in range(4):
            empty(("qiT", m), qiT[:, m, :])
        for n, (q, h) in enumerate((q, h) for q in QBS for h in range(NI)):
            w = (q + 1) * P
            b = full_s(act, ("dot", q, h))
            if n >= 4:
                q0, h0 = QBS[(n - 4) // NI], (n - 4) % NI
                act.wait_ge(scored, scores_until(q0, h0))
            act.activation(relu[:, n % 4, 0:w], b[:, 0:w], ACT.Relu).then_inc(s_emptied, 1)
        for b in range(MB):
            empty(("vm", b), vm[:, b, :], view=lambda b: b[:, 0:MH * HD])
        for m in range(4):
            empty(("qT", m), qT[:, m, :])
        for m in range(2):
            empty(("qm", m), qmT[:, m, :], scale=HD ** -0.5)
        for b in range(TB):
            for j in range(2):
                empty(("ml", b, j), lm[:, b, 2 * j:2 * j + 2, :], view=lambda b: b[:, :].rearrange("p (i m) -> p i m", i=2))

        def mem_exps(b):
            act.wait_ge(mem_soft, 2 * (b + 1))
            for i in range(MH):
                act.activation(lm[:, b, i, :], lm[:, b, i, :], ACT.Exp, bias=mmax[:, b, i:i + 1],
                               accum_out=msum[:, b, i:i + 1]).then_inc(mem_exp, 1)

        for c in range(2):
            empty(("gc", c), gcT[:, c, :])
            empty(("gb", c), gbT[:, c, :])
            if c == 0:
                for b in range(TB):
                    mem_exps(b)
        for h in range(H):
            empty(("ql", h), qlT[:, h, :], scale=HD ** -0.5)

        def mem_outputs():
            for b in range(TB):
                for m in range(MB):
                    empty(("pmT", b, m), pmT[:, m, :, b * P:(b + 1) * P], view=four)
            act.wait_ge(scored, scores_until(QBS[-1], NI - 1))
            for j in range(2):
                empty(("yc", j), mixT[:, 6 + j, :])

        def att_exps(i):
            q, g = units[i]
            w = (q + 1) * P
            act.wait_ge(soft, att_steps(i, 5))
            for h in range(4):
                act.activation(lg[:, i % 2, h, 0:w], lg[:, i % 2, h, 0:w], ACT.Exp, bias=amax[:, i, h:h + 1],
                               accum_out=asum[:, i, h:h + 1]).then_inc(att_exp, 1)

        mem_outputs()
        att_exps(0)
        for i, (q, g) in enumerate(units):
            if i + 1 < len(units):
                att_exps(i + 1)
            if i == 0:
                act.wait_ge(conv, 2 * CONV)
            for s in range(q + 1):
                if i:
                    act.wait_ge(s_filled, NO_S[("ol", *units[i - 1])] + 1)
                empty(("pT", q, g, s), pT[:, s, :])
            empty(("ol", q, g), olT[:, 4 * g:4 * g + 4, q * P:(q + 1) * P], view=four)
        for m in range(4):
            empty(("ya", m), mixT[:, m, :])
        def ln_root(b):
            act.wait_ge(ln1, LN * b + 4)
            act.activation(rstd[:, b:b + 1], rstd[:, b:b + 1], ACT.Sqrt).then_inc(root1, 1)

        def scores_of(b):
            empty(("x1T", b, 0), x1T[:, 0:4, b * P:(b + 1) * P], view=four)
            bk = full_s(act, ("rt", b))
            act.activation(sg_r[:, b, :], bk[:, 0:E], ACT.Sigmoid).then_inc(s_emptied, 1)

        def shared_silu(b):
            act.wait_ge(v_filled, NO_V["gu", b] + 1)
            if b:
                emptied_v(act, ("gu", b - 1))
            act.activation(sh_sg[:, :], bank[RING + NO_V["gu", b] % RING][:, 0:FE], ACT.Silu).then_inc(sh_silu, 1)

        def shared_hT(b):
            bk = full_s(act, ("shT", b))
            if b >= 2:
                act.wait_ge(v_filled, NO_V["yd", b - 2, 1] + 1)
            act.activation(sh_hT[:, b % 2, :, :], bk[:, 0:2 * P].rearrange("p (k t) -> p k t", k=2), ACT.Copy).then_inc(s_emptied, 1)

        for b in range(TB):
            ln_root(b)
            if b + 1 < TB:
                scores_of(b)
        shared_silu(0)
        scores_of(TB - 1)
        shared_silu(1)
        shared_hT(0)
        shared_silu(2)
        shared_silu(3)
        for b in range(1, TB):
            shared_hT(b)

        def finish_y(e, n, first=False):
            act.wait_ge(down_summed, e * 2 + 1)
            if not first:
                act.wait_ge(scattered[n % 2], y_free(e, n))
            act.activation(y[n % 2][0:CAP, 0:512], bank[5][0:CAP, :], ACT.Copy, scale=slot_weight(n % UNROLL)).then_inc(y_s, 1)

        def transpose_x(e, n):
            act.wait_ge(xgT_summed, e * 2 + 1)
            act.activation(xgT[n % 2][:, 0:4, :], slots4(bank[2]), ACT.Copy).then_inc(xgT_s, 1)

        def expert(e, n, first=False, last=False):
            act.wait_ge(gu_summed, e + 1)
            if not first:
                act.wait_ge(h_made, e)
            act.activation(sg[0:CAP, :], bank[0][0:CAP, 0:FE], ACT.Silu).then_inc(silu_made, 1)
            if not last:
                transpose_x(e + 1, n + 1)
            if not first:
                finish_y(e - 1, n - 1, first=isinstance(e, int) and e - 1 < 2)
            act.wait_ge(hT_summed, e + 1)
            act.activation(hT[:, :, :], slots4(bank[4])[:, 0:2, :], ACT.Copy).then_inc(hT_made, 1)

        transpose_x(0, 0)
        run_experts(act, expert)
        finish_y(E - 1, E - 1)
        act.wait_ge(over["shift"], 1)
        most = act.value_load(cnt_i[0:1, 0:1], min_val=0, max_val=T)
        with act.If(most > CAP):
            with act.Fori(0, (ROUNDS - 1) * E) as n:
                act.wait_ge(over["xgTp"], n * 2 + 1)
                act.activation(xgT[0][:, 0:4, :], slots4(bank[2]), ACT.Copy).then_inc(over["xgTs"], 1)
                act.wait_ge(over["gu"], n + 1)
                act.activation(sg[0:CAP, :], bank[0][0:CAP, 0:FE], ACT.Silu).then_inc(over["silu"], 1)
                act.wait_ge(over["hTp"], n + 1)
                act.activation(hT[:, :, :], slots4(bank[4])[:, 0:2, :], ACT.Copy).then_inc(over["hT"], 1)
                act.wait_ge(over["dn"], n * 2 + 1)
                act.activation(y[0][0:CAP, 0:512], bank[5][0:CAP, :], ACT.Copy, scale=slot_weight(0)).then_inc(over["ys"], 1)
        for b in range(TB):
            act.wait_ge(summed, FINAL * b + 2 + 4)
            act.activation(rstd2[:, b:b + 1], rstd2[:, b:b + 1], ACT.Sqrt).then_inc(root2, 1)

    @block.vector
    def _(dve):
        def empty(f, dst, view=None):
            b = full_v(dve, f)
            dve.tensor_copy(dst, view(b) if view else b[:, :]).then_inc(v_emptied, 1)

        def layer_norm(src, dst, stats, mean_var, r, gain, bias, done, start, root, roots):
            for c in range(2):
                dve.bn_stats(stats[:, c, :], src[:, c * 512:(c + 1) * 512]).then_inc(done, 1)
            dve.wait_ge(done, start + 2)
            dve.bn_aggr(mean_var, stats).then_inc(done, 1)
            dve.wait_ge(done, start + 3)
            dve.tensor_scalar(r, mean_var[:, 1:2], LN_EPS, None, ALU.add).then_inc(done, 1)
            dve.wait_ge(root, roots)
            dve.reciprocal(r, r).then_inc(done, 1)
            dve.wait_ge(done, start + 5)
            dve.tensor_scalar(src, src, mean_var[:, 0:1], r, ALU.subtract, ALU.mult).then_inc(done, 1)
            dve.wait_ge(done, start + 6)
            dve.tensor_tensor(src, src, gain, ALU.mult).then_inc(done, 1)
            dve.wait_ge(done, start + 7)
            dve.tensor_tensor(dst, src, bias, ALU.add).then_inc(done, 1)

        empty(("bias", 0), rv[0:H, 0:512], view=lambda b: b[0:H, :])
        empty(("bias", 1), rv[0:H, 512:SKEW], view=lambda b: b[0:H, 0:SKEW - 512])
        four = lambda b: b[:, :].rearrange("p (k t) -> p k t", k=4)
        for b in range(TB):
            empty(("xT", b, 1), xT[:, 4:8, b * P:(b + 1) * P], view=four)
        for b in range(MB):
            empty(("memT", b, 1), memT[:, 4:8, b * P:(b + 1) * P], view=four)
        for b in range(TB):
            bk = full_v(dve, ("proj", b))
            dve.tensor_copy(proj[:, b, :], bk[:, 0:QR + KVR])
            dve.tensor_copy(kk[:, b, :, :], bk[:, QR + KVR:QR + KVR + IDX].unsqueeze(1).to_broadcast([P, 2, IDX]))
            dve.tensor_scalar(iw[:, b, :], bk[:, QR + KVR + IDX:TOKEN_COLS], NI ** -0.5 * IDX ** -0.5, None,
                              ALU.mult).then_inc(v_emptied, 1)
        dve.wait_ge(squares, 2 * TB)
        for k, n in enumerate((QR, KVR)):
            dve.tensor_scalar(rms[:, k, :], ss[:, k, :], 1.0 / n, RMS_EPS, ALU.mult, ALU.add).then_inc(normed, 1)
        dve.wait_ge(squares, 2 * TB + 1)
        dve.reciprocal(rms[:, :, :], rms[:, :, :]).then_inc(normed, 1)
        dve.wait_ge(normed, 3)
        wait_dma(dve, "gq")
        wait_dma(dve, "gkv")
        for b in range(TB):
            dve.scalar_tensor_tensor(proj[:, b, 0:QR], proj[:, b, 0:QR], rms[:, 0, b:b + 1], gq[:, :],
                                     ALU.mult, ALU.mult).then_inc(normed, 1)
            dve.scalar_tensor_tensor(ckvn[:, b, :], proj[:, b, QR:QR + KVR], rms[:, 1, b:b + 1], gkv[:, :],
                                     ALU.mult, ALU.mult).then_inc(normed, 1)
        for q in QBS:
            w = (q + 1) * P
            sq = sel[:, q - 1, 0:w]
            for h in range(NI):
                emptied_s(dve, ("dot", q, h))
                r = relu[:, NO_S["dot", q, h] - NO_S["dot", QBS[0], 0] & 3, 0:w]
                if h == 0:
                    dve.tensor_scalar(sq, r, iw[:, q, 0:1], None, ALU.mult).then_inc(scored, 1)
                else:
                    dve.wait_ge(scored, scores_until(q, h - 1))
                    dve.scalar_tensor_tensor(sq, r, iw[:, q, h:h + 1], sq, ALU.mult, ALU.add).then_inc(scored, 1)
            dve.wait_ge(scored, scores_until(q, NI - 1))
            dve.wait_ge(constants, 4)
            dve.tensor_tensor(sel[:, q - 1, q * P:w], sel[:, q - 1, q * P:w], causal[:, :], ALU.add).then_inc(scored, 1)
        dve.wait_ge(scored, len(QBS) * (NI + 1))
        for r in range(TOPK // 8):
            for n, q in enumerate(QBS):
                if r:
                    dve.wait_ge(chosen, chosen_after(r - 1, 1, n))
                dve.max(top8[:, n, :], sel[:, q - 1, 0:(q + 1) * P]).then_inc(chosen, 1)
            for n, q in enumerate(QBS):
                sq = sel[:, q - 1, 0:(q + 1) * P]
                dve.wait_ge(chosen, chosen_after(r, 0, n))
                dve.match_replace(sq, top8[:, n, :], sq, TAKEN).then_inc(chosen, 1)
        for n, q in enumerate(QBS):
            sq = sel[:, q - 1, 0:(q + 1) * P]
            dve.wait_ge(chosen, chosen_after(TOPK // 8 - 1, 1, n))
            dve.tensor_scalar(sq, sq, MIDWAY, NEG, ALU.is_ge, ALU.mult).then_inc(chosen, 1)

        def mem_max(b):
            emptied_s(dve, ("ml", b, 1))
            dve.reduce_max(mmax[:, b, :], lm[:, b, :, :], AX.X).then_inc(mem_soft, 1)
            dve.wait_ge(mem_soft, 2 * b + 1)
            dve.tensor_scalar(mmax[:, b, :], mmax[:, b, :], -1.0, None, ALU.mult).then_inc(mem_soft, 1)

        def mem_norm(b):
            dve.wait_ge(mem_exp, MH * (b + 1))
            dve.reciprocal(msum[:, b, :], msum[:, b, :]).then_inc(mem_soft, 1)
            dve.wait_ge(mem_soft, 2 * TB + 2 * b + 1)
            dve.tensor_tensor(lm[:, b, :, :], lm[:, b, :, :], msum[:, b, :].unsqueeze(2).to_broadcast([P, MH, M]),
                              ALU.mult).then_inc(mem_soft, 1)

        def convolution(c):
            dve.memset(u[:, c, 0:2], 0.0)
            emptied_s(dve, ("gc", c))
            bk = full_v(dve, ("hc", c))
            dve.tensor_tensor(u[:, c, 2:], gcT[:, c, :], bk[:, :], ALU.mult).then_inc(v_emptied, 1)
            emptied_v(dve, ("hc", c))
            dve.tensor_scalar(cv[:, c, :], u[:, c, 0:T], cw[:, c, 0:1], None, ALU.mult).then_inc(conv, 1)
            for j in (1, 2):
                dve.wait_ge(conv, CONV * c + j)
                dve.scalar_tensor_tensor(cv[:, c, :], u[:, c, j:j + T], cw[:, c, j:j + 1], cv[:, c, :],
                                         ALU.mult, ALU.add).then_inc(conv, 1)
            dve.wait_ge(conv, CONV * c + 3)
            emptied_s(dve, ("gb", c))
            dve.tensor_tensor(mixT[:, 4 + c, :], cv[:, c, :], gbT[:, c, :], ALU.mult).then_inc(conv, 1)

        for b in range(TB):
            mem_max(b)
        wait_dma(dve, "cw", 6)
        convolution(0)
        for b in range(TB):
            mem_norm(b)
        convolution(1)

        wait_dma(dve, "bias")

        def bias_of(h, w):
            return B[:, h, w - 1::-1]

        def att_max(i):
            q, g = units[i]
            w = (q + 1) * P
            mask = causal[:, :] if q == 0 else sel[:, q - 1, 0:w]
            if i >= 2:
                dve.wait_ge(s_filled, NO_S[("pT", *units[i - 2], units[i - 2][0])] + 1)
            for h in range(4):
                bk = full_v(dve, ("lg", q, g, h))
                dve.tensor_tensor(lg[:, i % 2, h, 0:w], bias_of(4 * g + h, w), bk[:, 0:w], ALU.add).then_inc(v_emptied, 1)
            for h in range(4):
                emptied_v(dve, ("lg", q, g, h))
                dve.tensor_tensor_reduce(out=lg[:, i % 2, h, 0:w], in0=lg[:, i % 2, h, 0:w], in1=mask, scale=1.0,
                                         scalar=-3.4e38, op0=ALU.add, op1=ALU.max,
                                         accum_out=amax[:, i, h:h + 1]).then_inc(soft, 1)
            dve.wait_ge(soft, att_steps(i, 4))
            dve.tensor_scalar(amax[:, i, :], amax[:, i, :], -1.0, None, ALU.mult).then_inc(soft, 1)

        def att_norm(i):
            q, g = units[i]
            w = (q + 1) * P
            dve.wait_ge(att_exp, 4 * (i + 1))
            dve.reciprocal(asum[:, i, :], asum[:, i, :]).then_inc(soft, 1)
            dve.wait_ge(soft, att_steps(i, 6))
            for h in range(4):
                dve.tensor_scalar(lg[:, i % 2, h, 0:w], lg[:, i % 2, h, 0:w], asum[:, i, h:h + 1], None,
                                  ALU.mult).then_inc(soft, 1)

        att_max(0)
        for i in range(len(units)):
            if i + 1 < len(units):
                att_max(i + 1)
            att_norm(i)
        wait_dma(dve, "g1")
        wait_dma(dve, "b1")
        def residual(b, j):
            bk = full_v(dve, ("mo", b, j))
            xs = X[:, b, j * 512:(j + 1) * 512]
            dve.scalar_tensor_tensor(xs, xs, ALPHA, bk[:, :], ALU.mult, ALU.add).then_inc(v_emptied, 1)

        def first_norm(b):
            emptied_v(dve, ("mo", b, 1))
            layer_norm(X[:, b, :], X[:, b, :], bn[:, b, :, :], mv[:, b, :], rstd[:, b:b + 1], g1[:, :], b1[:, :],
                       ln1, LN * b, root1, b + 1)

        def x1_half(b):
            empty(("x1T", b, 1), x1T[:, 4:8, b * P:(b + 1) * P], view=four)

        steps = [0]

        def step(ins):
            ins.then_inc(routed, 1)
            steps[0] += 1

        def after():
            dve.wait_ge(routed, steps[0])

        by_group = lambda t, b: t[:, b, :].rearrange("p (g j) -> p g j", g=G)

        def route(b):
            emptied_s(dve, ("rt", b))
            step(dve.tensor_tensor(sc[:, b, :], sg_r[:, b, :], rb[:, :], ALU.add))
            after()
            for g in range(G):
                step(dve.max(g8[:, b, g, :], sc[:, b, g * EG:(g + 1) * EG]))
            after()
            step(dve.tensor_tensor(gs[:, b, :], g8[:, b, :, 0], g8[:, b, :, 1], ALU.add))
            after()
            step(dve.max(gtop[:, b, :], gs[:, b, :]))
            after()
            step(dve.max_index(gidx[:, b, :], gtop[:, b, :], gs[:, b, :]))
            after()
            step(dve.tensor_copy(gif[:, b, :], gidx[:, b, :]))
            after()
            step(dve.tensor_tensor(gcmp[:, b, :, :], giota[:, :].unsqueeze(2).to_broadcast([P, G, TOPG]),
                                   gif[:, b, 0:TOPG].unsqueeze(1).to_broadcast([P, G, TOPG]), ALU.is_equal))
            after()
            step(dve.tensor_reduce(gmask[:, b, :], gcmp[:, b, :, :], AX.X, ALU.add))
            after()
            step(dve.tensor_tensor(by_group(cand, b), by_group(sc, b), gmask[:, b, :].unsqueeze(2).to_broadcast([P, G, EG]), ALU.mult))
            after()
            step(dve.tensor_scalar(gmask[:, b, :], gmask[:, b, :], -1.0, -NEG, ALU.add, ALU.mult))
            after()
            step(dve.tensor_tensor(by_group(cand, b), by_group(cand, b), gmask[:, b, :].unsqueeze(2).to_broadcast([P, G, EG]), ALU.add))
            after()
            step(dve.max(etop[:, b, :], cand[:, b, :]))
            after()
            step(dve.match_replace(cand[:, b, :], etop[:, b, :], cand[:, b, :], TAKEN))
            after()
            step(dve.tensor_scalar(taken[:, b, :], cand[:, b, :], MIDWAY, None, ALU.is_lt))
            after()
            assert steps[0] == ROUTE * b + TAKEN_STEP
            step(dve.tensor_tensor(wts[:, b, :], sg_r[:, b, :], taken[:, b, :], ALU.mult))
            step(dve.tensor_scalar(tab[:, b, :, 0], taken[:, b, :], 0.0, tok[:, b:b + 1], ALU.mult, ALU.add))
            after()
            step(dve.reduce_sum(wsum[:, b:b + 1], wts[:, b, :], AX.X))
            after()
            step(dve.reciprocal(wrec[:, b:b + 1], wsum[:, b:b + 1]))
            after()
            step(dve.tensor_scalar(tab[:, b, :, 1], wts[:, b, :], wrec[:, b:b + 1], 2.5, ALU.mult, ALU.mult))

        def shared_mul(b):
            bk = full_v(dve, ("gu", b))
            dve.wait_ge(sh_silu, b + 1)
            dve.tensor_tensor(sh_h[:, b, :], sh_sg[:, :], bk[:, FE:2 * FE], ALU.mult).then_inc(v_emptied, 1)

        def shared_add(b):
            for j in range(2):
                bk = full_v(dve, ("yd", b, j))
                dve.scalar_tensor_tensor(sh_acc[:, b, j * 512:(j + 1) * 512], X[:, b, j * 512:(j + 1) * 512], ALPHA, bk[:, :],
                                         ALU.mult, ALU.add).then_inc(v_emptied, 1)

        def slots_of(e, dst, done):
            dve.tensor_tensor(dst[:, :, :], iota_c[:, :].unsqueeze(1).to_broadcast([P, TB, CAP]),
                              posm[:, :, bass.ds(e, 1)].to_broadcast([P, TB, CAP]), ALU.is_equal).then_inc(done, 1)

        dve.wait_ge(tables, 6)
        dve.tensor_scalar(tok[:, :], tok[:, :], -FAR, None, ALU.add).then_inc(tables, 1)
        dve.wait_ge(tables, 7)
        wait_dma(dve, "g1")
        wait_dma(dve, "b1")
        wait_dma(dve, "rb")
        for b in range(TB):
            residual(b, 0)
            if b:
                x1_half(b - 1)
            if b >= 2:
                route(b - 2)
            residual(b, 1)
            first_norm(b)
        route(TB - 2)
        shared_mul(0)
        x1_half(TB - 1)
        route(TB - 1)
        shared_mul(1)
        shared_add(0)
        bk = full_v(dve, ("pos",))
        dve.scalar_tensor_tensor(posm[:, :, :], bk[:, 0:TB * E].rearrange("p (b e) -> p b e", b=TB), 1.0, taken[:, :, :],
                                 ALU.add, ALU.mult).then_inc(v_emptied, 1)
        emptied_v(dve, ("pos",))
        step(dve.tensor_scalar(posm[:, :, :], posm[:, :, :], -1.0, None, ALU.add))
        after()
        for e in range(AHEAD):
            slots_of(e, oh[e], oh_made)
        bk = full_v(dve, ("cnt",))
        dve.reduce_max(cnt[:, :], bk[:, 0:E], AX.X).then_inc(v_emptied, 1)
        emptied_v(dve, ("cnt",))
        step(dve.tensor_copy(cnt_i[:, :], cnt[:, :]))
        shared_mul(2)
        bk = full_v(dve, ("slots",))
        dve.tensor_copy(w_slot[0:CAP, 0:AHEAD], bk[0:CAP, 1:2 * AHEAD:2])
        dve.tensor_scalar(idx_u[0:CAP, 0:AHEAD], bk[0:CAP, 0:2 * AHEAD:2], FAR, None, ALU.add).then_inc(v_emptied, 1)
        shared_mul(3)
        for b in range(1, TB):
            shared_add(b)

        def indices(buf, done):
            dve.tensor_copy(slot_weight(buf), bank[1][0:CAP, 1:2]).then_inc(done, 1)
            dve.tensor_scalar(idx_u[0:CAP, buf:buf + 1], bank[1][0:CAP, 0:1], FAR, None, ALU.add).then_inc(done, 1)

        def finish_y(e, n, first=False):
            dve.wait_ge(down_summed, e * 2 + 2)
            if not first:
                dve.wait_ge(scattered[n % 2], y_free(e, n))
            dve.tensor_scalar(y[n % 2][0:CAP, 512:1024], bank[6][0:CAP, :], slot_weight(n % UNROLL), None, ALU.mult).then_inc(y_v, 1)

        def transpose_x(e, n):
            dve.wait_ge(xgT_summed, e * 2 + 2)
            dve.tensor_copy(xgT[n % 2][:, 4:8, :], slots4(bank[3])).then_inc(xgT_v, 1)

        def make_slots(e, n):
            if not isinstance(e, int) or e >= 2 * AHEAD:
                dve.wait_ge(idx_summed, e - (2 * AHEAD - 1))
            slots_of(e, oh[n % AHEAD], oh_made)

        def make_indices(e, n):
            dve.wait_ge(idx_summed, e - (AHEAD - 1))
            indices(n % UNROLL, idx_made)

        def expert(e, n, first=False, last=False):
            tail = isinstance(e, int) and e >= E - AHEAD
            if not first and not (tail and e + AHEAD - 1 >= E):
                make_indices(e + (AHEAD - 1), n + AHEAD - 1)
            dve.wait_ge(silu_made, e + 1)
            if not first:
                dve.wait_ge(hT_summed, e)
            dve.tensor_tensor(h_sb[0:CAP, :], sg[0:CAP, :], bank[0][0:CAP, FE:2 * FE], ALU.mult).then_inc(h_made, 1)
            if not last:
                transpose_x(e + 1, n + 1)
            if not tail:
                make_slots(e + AHEAD, n + AHEAD)
            if not first:
                finish_y(e - 1, n - 1, first=isinstance(e, int) and e - 1 < 2)

        transpose_x(0, 0)
        run_experts(dve, expert)
        finish_y(E - 1, E - 1)
        dve.engine_nop().then_inc(over["shift"], 1)
        most = dve.value_load(cnt_i[0:1, 0:1], min_val=0, max_val=T)
        with dve.If(most > CAP):
            for i in range(2):
                dve.wait_ge(scattered[i], 16 * (E // 2))
            with dve.Fori(1, ROUNDS) as r:
                dve.tensor_scalar(posm[:, :, :], posm[:, :, :], -float(CAP), None, ALU.add).then_inc(over["shift"], 1)
                with dve.Fori(0, E) as e:
                    n = (r - 1) * E + e
                    dve.wait_ge(over["shift"], r + 1)
                    slots_of(e, oh[0], over["oh"])
                    dve.wait_ge(over["idxp"], n + 1)
                    indices(0, over["idx"])
                    dve.wait_ge(over["xgTp"], n * 2 + 2)
                    dve.tensor_copy(xgT[0][:, 4:8, :], slots4(bank[3])).then_inc(over["xgTv"], 1)
                    dve.wait_ge(over["silu"], n + 1)
                    dve.tensor_tensor(h_sb[0:CAP, :], sg[0:CAP, :], bank[0][0:CAP, FE:2 * FE], ALU.mult).then_inc(over["h"], 1)
                    dve.wait_ge(over["dn"], n * 2 + 2)
                    dve.tensor_scalar(y[0][0:CAP, 512:1024], bank[6][0:CAP, :], slot_weight(0), None, ALU.mult).then_inc(over["yv"], 1)
                    dve.wait_ge(over["sc"], n * 16 + 16)
        wait_dma(dve, "g2")
        wait_dma(dve, "b2")
        for b in range(TB):
            dve.wait_ge(rows_loaded[b], 32)
            for i in range(2):
                if i:
                    dve.wait_ge(summed, FINAL * b + i)
                dve.tensor_tensor(sh_acc[:, b, :], sh_acc[:, b, :], yr[:, b, i, :], ALU.add).then_inc(summed, 1)
            dve.wait_ge(summed, FINAL * b + 2)
            layer_norm(sh_acc[:, b, :], sh_acc[:, b, :], bn2[:, b, :, :], mv2[:, b, :], rstd2[:, b:b + 1], g2[:, :], b2[:, :],
                       summed, FINAL * b + 2, root2, b + 1)

    @block.tensor
    def _(pe):
        def mm(dst, lhsT, rhs, start, stop):
            return pe.matmul(dst, lhsT, rhs, start=start, stop=stop)

        def transposes(dst, srcs):
            for i, s in enumerate(srcs):
                last = pe.transpose(dst[:, i * P:i * P + s.shape[0]], s, ident[0:s.shape[0], 0:s.shape[0]])
            return last

        def summed(dst, pairs):
            for i, (l, r) in enumerate(pairs):
                last = mm(dst, l, r, i == 0, i == len(pairs) - 1)
            return last

        wait_dma(pe, "bucket")
        wait_dma(pe, "rel")
        for n, (lo, hi) in enumerate(((0, 512), (512, SKEW))):
            b = fill_v(pe, ("bias", n))
            mm(b[0:H, 0:hi - lo], rel[0:BUCKETS, :], onehot[0:BUCKETS, lo:hi], True, True).then_inc(v_filled, 1)
        pe.wait_ge(constants, 3)
        for b in range(TB):
            wait_dma(pe, f"x{b}")
            cols = X[:, b, :].rearrange("p (c k) -> p k c", k=DK)
            transposes(fill_s(pe, ("xT", b, 0)), [cols[:, k, :] for k in range(4)]).then_inc(s_filled, 1)
            transposes(fill_v(pe, ("xT", b, 1)), [cols[:, k, :] for k in range(4, 8)]).then_inc(v_filled, 1)
        wait_dma(pe, "mem")
        for b in range(MB):
            cols = mem_sb[:, b, :].rearrange("p (c k) -> p k c", k=DK)
            transposes(fill_s(pe, ("memT", b, 0)), [cols[:, k, :] for k in range(4)]).then_inc(s_filled, 1)
            transposes(fill_v(pe, ("memT", b, 1)), [cols[:, k, :] for k in range(4, 8)]).then_inc(v_filled, 1)
        wait_dma(pe, "w_tok")
        for b in range(TB):
            emptied_s(pe, ("xT", b, 0))
            emptied_v(pe, ("xT", b, 1))
            summed(fill_v(pe, ("proj", b))[:, 0:TOKEN_COLS],
                   [(xT[:, k, b * P:(b + 1) * P], w_in[:, k, 0:TOKEN_COLS]) for k in range(DK)]).then_inc(v_filled, 1)
        emptied_s(pe, ("memT", MB - 1, 0))
        emptied_v(pe, ("memT", MB - 1, 1))
        wait_dma(pe, "wmk")
        for m in range(2):
            summed(fill_s(pe, ("kmT", m))[:, 0:M],
                   [(wmk[:, k, m * P:(m + 1) * P], memT[:, k, :]) for k in range(DK)]).then_inc(s_filled, 1)
        wait_dma(pe, "uk")
        transposes(fill_s(pe, ("ukT",)), [w_uk[:, m * P:(m + 1) * P] for m in range(4)]).then_inc(s_filled, 1)
        pe.wait_ge(normed, NORMED)
        for b in range(TB):
            transposes(fill_s(pe, ("cT", b)), [proj[:, b, 0:P], proj[:, b, P:2 * P], ckvn[:, b, :],
                                               kk[:, b, :, :].rearrange("p i d -> p (i d)")]).then_inc(s_filled, 1)
        emptied_s(pe, ("cT", TB - 1))
        wait_dma(pe, "qi")
        for m in range(4):
            summed(fill_s(pe, ("qiT", m))[:, :], [(w_qi[:, k, m * P:(m + 1) * P], latT[:, k, :]) for k in range(2)]).then_inc(s_filled, 1)
        for q in QBS:
            w = (q + 1) * P
            for h in range(NI):
                emptied_s(pe, ("qiT", h // 2))
                lo = h % 2 * IDX
                b = fill_s(pe, ("dot", q, h))
                mm(b[:, 0:w], qiT[lo:lo + IDX, h // 2, q * P:(q + 1) * P], latT[lo:lo + IDX, 3, 0:w], True, True).then_inc(s_filled, 1)

        def channels(dst, lo):
            return summed(dst[:, :], [(w_in[:, k, lo:lo + P], xT[:, k, :]) for k in range(DK)])

        wait_dma(pe, "wmv")
        for b in range(MB):
            summed(fill_s(pe, ("vm", b))[:, 0:MH * HD],
                   [(memT[:, k, b * P:(b + 1) * P], wmv[:, k, :]) for k in range(DK)]).then_inc(s_filled, 1)
        wait_dma(pe, "uq")
        for m in range(4):
            summed(fill_s(pe, ("qT", m))[:, :], [(w_uq[:, k, m * P:(m + 1) * P], latT[:, k, :]) for k in range(2)]).then_inc(s_filled, 1)
        wait_dma(pe, "w_chan")
        for m in range(2):
            channels(fill_s(pe, ("qm", m)), TOKEN_COLS + 3 * CC + m * P).then_inc(s_filled, 1)
        emptied_s(pe, ("qm", 1))
        emptied_s(pe, ("vm", MB - 1))
        for b in range(TB):
            for j in range(2):
                bk = fill_s(pe, ("ml", b, j))
                for i in range(2):
                    last = mm(bk[:, i * M:(i + 1) * M], qmT[j * HD:(j + 1) * HD, i, b * P:(b + 1) * P], kmT[j * HD:(j + 1) * HD, i, :], True, True)
                last.then_inc(s_filled, 1)
        for c in range(2):
            channels(fill_s(pe, ("gc", c)), TOKEN_COLS + CC + c * P).then_inc(s_filled, 1)
            channels(fill_v(pe, ("hc", c)), TOKEN_COLS + 2 * CC + c * P).then_inc(v_filled, 1)
            channels(fill_s(pe, ("gb", c)), TOKEN_COLS + c * P).then_inc(s_filled, 1)
        emptied_s(pe, ("qT", 3))
        for h in range(H):
            lo = h % 2 * HD
            mm(fill_s(pe, ("ql", h))[:, :], ukT[lo:lo + HD, h // 2, :], qT[lo:lo + HD, h // 2, :], True, True).then_inc(s_filled, 1)
        emptied_s(pe, ("ql", H - 1))

        def logits(i):
            q, g = units[i]
            w = (q + 1) * P
            for h in range(4):
                mm(fill_v(pe, ("lg", q, g, h))[:, 0:w], qlT[:, 4 * g + h, q * P:(q + 1) * P], latT[:, 2, 0:w], True, True).then_inc(v_filled, 1)

        logits(0)
        for b in range(TB):
            pe.wait_ge(mem_soft, 2 * TB + 2 * (b + 1))
            for m in range(MB):
                transposes(fill_s(pe, ("pmT", b, m)), [lm[:, b, s, m * P:(m + 1) * P] for s in range(MH)]).then_inc(s_filled, 1)
        emptied_s(pe, ("pmT", TB - 1, MB - 1))
        for i in range(2):
            bk = fill_s(pe, ("yc", i))
            for j in range(2):
                h = 2 * i + j
                for m in range(MB):
                    last = mm(bk[j * HD:(j + 1) * HD, :], vm[:, m, h * HD:(h + 1) * HD], pmT[:, m, 2 * j + i, :], m == 0, m == MB - 1)
            last.then_inc(s_filled, 1)
        logits(1)
        for i, (q, g) in enumerate(units):
            if i + 2 < len(units):
                logits(i + 2)
            pe.wait_ge(soft, att_steps(i, UNIT))
            for s in range(q + 1):
                transposes(fill_s(pe, ("pT", q, g, s)), [lg[:, i % 2, h, s * P:(s + 1) * P] for h in range(4)]).then_inc(s_filled, 1)
            bk = fill_s(pe, ("ol", q, g))
            for s in range(q + 1):
                emptied_s(pe, ("pT", q, g, s))
                last = mm(bk[:, :], ckvn[:, s, :], pT[:, s, :], s == 0, s == q)
            last.then_inc(s_filled, 1)
        emptied_s(pe, ("ol", TB - 1, 1))
        for m in range(4):
            bk = fill_s(pe, ("ya", m))
            for j in range(2):
                h = 2 * m + j
                last = mm(bk[j * HD:(j + 1) * HD, :], w_uv[:, h * HD:(h + 1) * HD], olT[:, h, :], True, True)
            last.then_inc(s_filled, 1)
        wait_dma(pe, "w_out")
        emptied_s(pe, ("ya", 3))
        pe.wait_ge(conv, 2 * CONV)
        def output(b, j):
            summed(fill_v(pe, ("mo", b, j))[:, :],
                   [(mixT[:, k, b * P:(b + 1) * P], w_out[:, k, j * 512:(j + 1) * 512]) for k in range(DK)]).then_inc(v_filled, 1)

        def x1_transposed(b):
            pe.wait_ge(ln1, LN * (b + 1))
            cols = X[:, b, :].rearrange("p (c k) -> p k c", k=DK)
            transposes(fill_s(pe, ("x1T", b, 0)), [cols[:, k, :] for k in range(4)]).then_inc(s_filled, 1)
            transposes(fill_v(pe, ("x1T", b, 1)), [cols[:, k, :] for k in range(4, 8)]).then_inc(v_filled, 1)

        def router_logits(b):
            emptied_s(pe, ("x1T", b, 0))
            emptied_v(pe, ("x1T", b, 1))
            summed(fill_s(pe, ("rt", b))[:, 0:E], [(x1T[:, k, b * P:(b + 1) * P], w_rt[:, k, :]) for k in range(DK)]).then_inc(s_filled, 1)

        def gate_up(dst, xt, w):
            return summed(dst, [(xt[:, k, :], w[:, :, k, :]) for k in range(DK)])

        def shared_up(b):
            gate_up(fill_v(pe, ("gu", b))[:, :], x1T[:, :, b * P:(b + 1) * P], sh_gu).then_inc(v_filled, 1)

        def shared_down(b):
            emptied_v(pe, ("gu", b))
            hh = sh_h[:, b, :].rearrange("p (c k) -> p k c", k=2)
            transposes(fill_s(pe, ("shT", b)), [hh[:, k, :] for k in range(2)]).then_inc(s_filled, 1)
            emptied_s(pe, ("shT", b))
            for j in range(2):
                summed(fill_v(pe, ("yd", b, j))[:, :], [(sh_hT[:, b % 2, k, :], sh_d[:, k, j * 512:(j + 1) * 512]) for k in range(2)]).then_inc(v_filled, 1)

        def slot_table(dst, e, buf):
            return summed(dst, [(oh[buf][:, b, :], tab[:, b, bass.ds(e, 1), :].rearrange("p e c -> p (e c)")) for b in range(TB)])

        output(0, 0)
        output(0, 1)
        wait_dma(pe, "rt")
        for b in range(1, TB):
            output(b, 0)
            x1_transposed(b - 1)
            output(b, 1)
            router_logits(b - 1)
        wait_dma(pe, "sh", 3)
        shared_up(0)
        x1_transposed(TB - 1)
        router_logits(TB - 1)
        shared_up(1)
        shared_down(0)
        pe.wait_ge(routed, ROUTE * (TB - 1) + TAKEN_STEP)
        bk = fill_v(pe, ("pos",))
        for b in range(TB):
            last = summed(bk[:, b * E:(b + 1) * E], [(ones[:, :], taken[:, k, :]) for k in range(b)] + [(tri[:, :], taken[:, b, :])])
        last.then_inc(v_filled, 1)
        summed(fill_v(pe, ("cnt",))[:, 0:E], [(ones[:, :], taken[:, k, :]) for k in range(TB)]).then_inc(v_filled, 1)
        shared_up(2)
        pe.wait_ge(oh_made, AHEAD)
        bk = fill_v(pe, ("slots",))
        for e in range(AHEAD):
            last = slot_table(bk[0:CAP, 2 * e:2 * e + 2], e, e)
        last.then_inc(v_filled, 1)
        shared_up(3)
        for b in range(1, TB):
            shared_down(b)

        pe.wait_ge(s_emptied, len(FILLS_S))
        pe.wait_ge(v_emptied, len(FILLS_V))

        def tokens(buf, done):
            cols = xg[buf][0:CAP, :].rearrange("p (c k) -> p k c", k=DK)
            transposes(bank[2], [cols[:, k, :] for k in range(4)]).then_inc(done, 1)
            transposes(bank[3], [cols[:, k, :] for k in range(4, 8)]).then_inc(done, 1)

        h_cols = h_sb[0:CAP, :].rearrange("p (c k) -> p k c", k=2)

        def down(s, done):
            for j in range(2):
                summed(bank[5 + j][0:CAP, :], [(hT[:, k, :], Wd[s][:, k, j * 512:(j + 1) * 512]) for k in range(2)]).then_inc(done, 1)

        def tokens_e(e, n):
            pe.wait_ge(gathered[n % 4], (e - n % 4) * 4 + 16)
            if not (isinstance(e, int) and e == 0):
                pe.wait_ge(xgT_s, e)
                pe.wait_ge(xgT_v, e)
            tokens(n % 4, xgT_summed)

        def down_e(e, n, first=False):
            pe.wait_ge(hT_made, e + 1)
            if not first:
                pe.wait_ge(y_s, e)
                pe.wait_ge(y_v, e)
            down((n + 2) % SLOTS, down_summed)

        def table_e(e, n, first=False):
            pe.wait_ge(oh_made, e + 1)
            if not first:
                pe.wait_ge(idx_made, (e - AHEAD) * 2)
            slot_table(bank[1][0:CAP, 0:2], e, n % AHEAD).then_inc(idx_summed, 1)

        def expert(e, n, first=False, last=False):
            tail = isinstance(e, int) and e >= E - AHEAD
            s = (n + 2) % SLOTS
            pe.wait_ge(w_loaded[s], (e - n % SLOTS) * 12 + 48)
            pe.wait_ge(xgT_s, e + 1)
            pe.wait_ge(xgT_v, e + 1)
            if not first:
                pe.wait_ge(h_made, e)
            gate_up(bank[0][0:CAP, :], xgT[n % 2], Wgu[s]).then_inc(gu_summed, 1)
            if not last:
                tokens_e(e + 1, n + 1)
            if not first:
                down_e(e - 1, n - 1, first=isinstance(e, int) and e == 1)
            if not tail:
                table_e(e + AHEAD, n + AHEAD, first=first)
            pe.wait_ge(h_made, e + 1)
            if not first:
                pe.wait_ge(hT_made, e)
            transposes(bank[4], [h_cols[:, k, :] for k in range(2)]).then_inc(hT_summed, 1)

        tokens_e(0, 0)
        run_experts(pe, expert)
        down_e(E - 1, SLOTS - 1)
        pe.wait_ge(over["shift"], 1)
        most = pe.value_load(cnt_i[0:1, 0:1], min_val=0, max_val=T)
        with pe.If(most > CAP):
            with pe.Fori(1, ROUNDS) as r:
                with pe.Fori(0, E) as e:
                    n = (r - 1) * E + e
                    pe.wait_ge(over["oh"], n + 1)
                    slot_table(bank[1][0:CAP, 0:2], e, 0).then_inc(over["idxp"], 1)
                    pe.wait_ge(over["gat"], n * 16 + 16)
                    tokens(0, over["xgTp"])
                    pe.wait_ge(over["xgTs"], n + 1)
                    pe.wait_ge(over["xgTv"], n + 1)
                    pe.wait_ge(over["w"], n * 48 + 48)
                    gate_up(bank[0][0:CAP, :], xgT[0], Wgu[0]).then_inc(over["gu"], 1)
                    pe.wait_ge(over["h"], n + 1)
                    transposes(bank[4], [h_cols[:, k, :] for k in range(2)]).then_inc(over["hTp"], 1)
                    pe.wait_ge(over["hT"], n + 1)
                    down(0, over["dn"])


NAMES = ("x", "mem", "w_in", "q_norm_g", "kv_norm_g", "w_uq", "w_uk", "w_uv", "w_qidx", "rel_bias", "conv_w",
         "w_mem_k", "w_mem_v", "w_out", "ln1_g", "ln1_b", "w_router", "router_bias", "w_e_gate", "w_e_up",
         "w_e_down", "w_s_gate", "w_s_up", "w_s_down", "ln2_g", "ln2_b")


def kernel(**inputs):
    import concourse.bacc as bacc
    from concourse.bass_utils import run_bass_kernel_spmd

    nc = bacc.Bacc("TRN2", target_bir_lowering=False, num_devices=1)
    given = {n: np.ascontiguousarray(inputs[n]) for n in NAMES}
    given["buckets"] = bucket_table()
    arrays = {f"in_{n}": v for n, v in given.items()}
    aps = {n: nc.dram_tensor(f"in_{n}", v.shape, mybir.dt.from_np(v.dtype), kind="ExternalInput").ap() for n, v in given.items()}
    out = nc.dram_tensor("out_0", (1, T, D), F32, kind="ExternalOutput").ap()
    layer_kernel(nc, aps, out)
    r = run_bass_kernel_spmd(nc, [arrays], core_ids=[0])
    return r.results[0]["out_0"]
```

```python
import math
from contextlib import ExitStack

import concourse.bass as bass
import numpy as np
from concourse import mybir

F32 = mybir.dt.float32
BF16 = mybir.dt.bfloat16
F32R = mybir.dt.float32r
U32 = mybir.dt.uint32
I32 = mybir.dt.int32
ALU = mybir.AluOpType
ACT = mybir.ActivationFunctionType
AX = mybir.AxisListType

P = 128
T, D = 512, 1024
TB = T // P
DK = D // P
M = 256
MB = M // P
QR, KVR, IDX, NI = 256, 128, 64, 8
H, HD = 8, 64
CC = 256
MH = 4
TOKEN_COLS = QR + KVR + IDX + NI
IN_COLS = TOKEN_COLS + 3 * CC + MH * HD
TOPK = min(256, T // 4)
BUCKETS, MAX_DIST = 32, 128
E, G, TOPG, TOPE = 64, 8, 4, 8
EG = E // G
FE = 256
CAP = 96
ROUNDS = -(-T // CAP)
SLOTS = 4
AHEAD = 4
UNROLL = 8
SKEW = 640
ALPHA = 2.0 ** 0.25
LN_EPS, RMS_EPS = 1e-5, 1e-6
NEG = -3.0e38
TAKEN = -3.3e38
MIDWAY = -3.2e38
FAR = float(1 << 20)
HALF = T // 2
COLS = 5
KB = 1024
BASE = 16512

RING = 4
QBS = (3, 2, 1)
FILLS_S = (
    [("xT", b, 0) for b in range(TB)] + [("memT", b, 0) for b in range(MB)]
    + [("kmT", m) for m in range(2)]
    + [("ukT",)] + [("cT", b) for b in range(TB)] + [("qiT", m) for m in range(4)]
    + [("dot", q, h) for q in QBS for h in range(NI)]
    + [("vm", b) for b in range(MB)] + [("qT", m) for m in range(4)] + [("qm", m) for m in range(2)]
    + [("ml", b, j) for b in range(TB) for j in range(2)]
    + [(k, c) for c in range(2) for k in ("gc", "gb")]
    + [("ql", h) for h in range(H)]
    + [("pmT", b, m) for b in range(TB) for m in range(MB)] + [("yc", j) for j in range(2)]
    + [f for i in range(2 * TB) for f in [("pT", i // 2, i % 2, s) for s in range(i // 2 + 1)] + ([("ol", (i - 1) // 2, (i - 1) % 2)] if i else [])]
    + [("ol", TB - 1, 1)]
    + [("ya", m) for m in range(4)]
    + [f for b in range(TB) for f in (("x1T", b, 0), ("rt", b))]
    + [("shT", b) for b in range(TB)]
)
FILLS_V = (
    [("bias", n) for n in range(2)]
    + [("xT", 0, 1), ("xT", 1, 1), ("proj", 0), ("xT", 2, 1), ("proj", 1), ("xT", 3, 1), ("proj", 2)]
    + [("memT", 0, 1), ("proj", 3), ("memT", 1, 1)]
    + [("hc", c) for c in range(2)]
    + [("lg", q, g, h) for q in range(TB) for g in range(2) for h in range(4)]
    + [("mo", 0, 0), ("mo", 0, 1)] + [f for b in range(1, TB) for f in (("mo", b, 0), ("x1T", b - 1, 1), ("mo", b, 1))]
    + [("gu", 0), ("gu", 1), ("x1T", 3, 1), ("gu", 2), ("yd", 0, 0), ("yd", 0, 1)]
    + [("pos",), ("cnt",), ("gu", 3), ("slots",)]
    + [("yd", b, j) for b in range(1, TB) for j in range(2)]
)
NO_S = {f: n for n, f in enumerate(FILLS_S)}
NO_V = {f: n for n, f in enumerate(FILLS_V)}


def bucket_table():
    n = np.arange(T)
    exact = BUCKETS // 2
    far = np.log(np.maximum(n, 1).astype(np.float32) / np.float32(exact)) / np.float32(math.log(MAX_DIST / exact))
    bucket = np.where(n < exact, n, np.minimum(exact + (far * np.float32(BUCKETS - exact)).astype(np.int32), BUCKETS - 1))
    table = np.zeros((BUCKETS, SKEW), np.float32)
    table[bucket, n + P - 1] = 1.0
    return table


def layer_kernel(nc, a, out):
    with ExitStack() as ctx:
        build(nc, ctx, a, out)


def build(nc, ctx, a, out):
    def at(name, kb, *shape, dt=F32):
        return nc.alloc_sbuf_tensor_at(name, [P, *shape], dt, offset=BASE + int(kb * KB))

    def sem(name):
        return ctx.enter_context(nc.semaphore(name))

    def dram(name, *shape):
        return nc.dram_tensor(name, shape, F32, kind="Internal").ap()

    w_in = at("w_in", 0, DK, IN_COLS)
    w_out = at("w_out_sb", 0, DK, D)
    g1 = at("g1", 32, D)
    b1 = at("b1", 36, D)
    w_rt = at("w_rt", 40, DK, E)
    xT = at("xT", 48, DK, T)
    qlT = at("qlT", 48, H, T)
    mem_sb = at("mem_sb", 64, MB, D)
    memT = at("memT", 72, DK, M)
    wmk = at("wmk", 80, DK, MH * HD)
    wmv = at("wmv", 88, DK, MH * HD)
    lm = at("lm", 64, TB, MH, M)
    pmT = at("pmT", 80, MB, MH, T)
    olT = at("olT", 64, H, T)
    X = at("X", 96, TB, D)
    w_uq = at("w_uq_sb", 112, 2, H * HD)
    w_qi = at("w_qi", 116, 2, NI * IDX)
    relu = at("relu", 120, 4, T)
    mixT = at("mixT", 112, DK, T)
    x1T = at("x1T", 128, DK, T)
    B = at("B", 128, H, T)
    sh_acc = at("sh_acc", 112, TB, D)
    qT = at("qT", 144, 4, T)
    qiT = at("qiT", 152, 4, T)
    qmT = at("qmT", 152, 2, T)
    lg = [at(f"lg{i}", kb, 4, T) for i, kb in enumerate((144, 152, 80))]
    sel = at("sel", 160, 3, T)
    sh_w = at("sh_w", 144, 24 * KB // 4)
    proj = at("proj", 166, TB, QR + KVR)
    kk = at("kk", 172, TB, 2, IDX)
    gcT = at("gcT", 166, 2, T)
    gbT = at("gbT", 170, 2, T)
    u = at("u", 174, 2, T + 2)
    cv = at("cv", 178.125, 2, T)
    pT = [at("pT0", 168, 4, T), at("pT1", 88, 4, T)]
    latT = at("latT", 182.5, 4, T)
    ckvn = at("ckvn", 190.5, TB, KVR)
    w_uk = at("w_uk_sb", 192.5, H * HD)
    w_uv = at("w_uv_sb", 194.5, H * HD)
    ukT = at("ukT", 196.5, 4, P)
    kmT = at("kmT", 198.5, 2, M)
    vm = at("vm", 200.5, MB, MH * HD)
    onehot = at("onehot", 200.5, SKEW)
    gq = at("gq", 196.5, QR)
    gkv = at("gkv", 197.5, KVR)
    rel = at("rel", 198, H)
    square = at("square", 181, QR)
    rv = at("rv", 178.5, SKEW)
    ident = at("ident", 203, P)
    causal = at("causal", 203.5, P)
    small = 204.0
    ss = at("ss", small, 2, TB)
    rms = at("rms", small + .03125, 2, TB)
    iw = at("iw", small + .0625, TB, NI)
    top8 = at("top8", small + .875, 3, 8)
    cw = at("cw", small + .21875, 2, 3)
    mmax = at("mmax", small + .25, TB, MH)
    msum = at("msum", small + .3125, TB, MH)
    amax = at("amax", small + .375, 2 * TB, 4)
    asum = at("asum", small + .5, 2 * TB, 4)
    bn = at("bn", small + .625, TB, 2, 6)
    mv = at("mv", small + .8125, TB, 2)
    rstd = at("rstd", small + .84375, TB)
    zeros = at("zeros", 205, 256)
    W = [at(f"W{s}", 24 * s, 24 * KB // 4) for s in range(SLOTS)]
    xg = [at(f"xg{i}", kb, D) for i, kb in enumerate((128, 132, 160, 164))]
    xgT = [at(f"xgT{i}", 136 + 4 * i, DK, CAP) for i in range(2)]
    y = [at(f"y{i}", 144 + 4 * i, D) for i in range(2)]
    oh = [at(f"oh{i}", 182.5 + i, TB, CAP, dt=BF16) for i in range(AHEAD)]
    h_sb = at("h_sb", 156, FE)
    sg = at("sg", 157, FE)
    hT = at("hT", 158, 2, CAP)
    hT_hi = at("hT_hi", 158, 2, P, dt=F32R)
    hT_lo = at("hT_lo", 159, 2, P, dt=F32R)
    wd_hi = [at(f"wd_hi{i}", 96 + 8 * i, 2, D, dt=F32R) for i in range(2)]
    wd_lo = [at(f"wd_lo{s}", 24 * s + 16, 2, D, dt=F32R) for s in range(SLOTS)]
    sh_sg = at("sh_sg", 168, FE)
    sh_h = at("sh_h", 196.5, TB, FE)
    sh_hT = at("sh_hT", 200.5, 2, 2, P)
    sg_r = at("sg_r", 171, TB, E)
    sc = at("sc", 172, TB, E)
    rb = at("rb", 173, E)
    g8 = at("g8", 173.25, TB, G, 8)
    gs = at("gs", 174.25, TB, G)
    gtop = at("gtop", 174.375, TB, 8)
    gidx = at("gidx", 174.5, TB, 8, dt=U32)
    gif = at("gif", 174.625, TB, 8)
    gcmp = at("gcmp", 175, TB, G, TOPG)
    gmask = at("gmask", 175.5, TB, G)
    etop = at("etop", 175.625, TB, 8)
    cand = at("cand", 176, TB, E)
    taken = at("taken", 177, TB, E)
    wts = at("wts", 178, TB, E)
    wsum = at("wsum", 179, TB)
    wrec = at("wrec", 179.03125, TB)
    posm = at("posm", 179.5, TB, E)
    tri = at("tri", 190.5, P, dt=BF16)
    ones = at("ones", 190.75, P, dt=BF16)
    took = at("took", 191, TB, E, dt=BF16)
    iota_c = at("iota_c", 191.5, CAP)
    tok = at("tok", 192, TB)
    giota = at("giota", 192.0625, G)
    cnt = at("cnt", 192.125, 1)
    cnt_i = at("cnt_i", 192.15625, 1, dt=I32)
    idx_u = at("idx_u", 181.75, UNROLL, dt=U32)
    w_slot = at("w_slot", 182, UNROLL)
    tab = at("tab", 192.5, TB, E, COLS, dt=BF16)
    rest = at("rest", 186.5, TB, E)
    yr = [at(f"yr{i}", 48 + 16 * i, TB, D) for i in range(2)]
    g2 = at("g2", 168, D)
    b2 = at("b2", 152, D)
    bn2 = at("bn2", 173.5, TB, 2, 6)
    mv2 = at("mv2", 173.75, TB, 2)
    rstd2 = at("rstd2", 173.875, TB)

    bias_dram = dram("bias_rows", H, SKEW)
    x1_dram = dram("x1_rows", T, D)
    y_dram = [dram(f"y_rows{i}", T, D) for i in range(2)]

    bank = [ctx.enter_context(nc.psum_tensor(f"bank{i}", [P, 512], F32)) for i in range(8)]

    s_filled, s_emptied = sem("s_filled"), sem("s_emptied")
    v_filled, v_emptied = sem("v_filled"), sem("v_emptied")
    loaded = {n: sem(f"loaded_{n}") for n in (
        "x0", "x1", "x2", "x3", "w_tok", "w_chan", "mem", "wmk", "wmv", "uq", "qi", "uk", "uv", "bucket",
        "rel", "gq", "gkv", "cw", "bias", "w_out", "g1", "b1", "rt", "rb", "sh", "g2", "b2")}
    y_cleared = sem("y_cleared")
    bias_stored, x1_stored = sem("bias_stored"), sem("x1_stored")
    constants = sem("constants")
    squares = sem("squares")
    normed = sem("normed")
    scored = sem("scored")
    chosen = sem("chosen")
    mem_soft = sem("mem_soft")
    mem_exp = sem("mem_exp")
    conv = sem("conv")
    soft = sem("soft")
    att_exp = sem("att_exp")
    ln1 = sem("ln1")
    root1 = sem("root1")
    routed = sem("routed")
    tables = sem("tables")
    sh_silu = sem("sh_silu")

    w_loaded = [sem(f"w_loaded{s}") for s in range(SLOTS)]
    oh_made = sem("oh_made")
    idx_summed = sem("idx_summed")
    idx_made = sem("idx_made")
    pool_turns = sem("pool_turns")
    xg_clear = sem("xg_clear")
    gathered = [sem(f"gathered{i}") for i in range(4)]
    scattered = [sem(f"scattered{i}") for i in range(2)]
    xgT_summed = sem("xgT_summed")
    xgT_s, xgT_v = sem("xgT_s"), sem("xgT_v")
    gu_summed = sem("gu_summed")
    silu_made = sem("silu_made")
    h_made = sem("h_made")
    hT_summed = sem("hT_summed")
    hi_made, lo_made = sem("hi_made"), sem("lo_made")
    hT_padded = sem("hT_padded")
    hT_hi_made, hT_lo_made = sem("hT_hi_made"), sem("hT_lo_made")
    down_summed = sem("down_summed")
    y_s, y_v = sem("y_s"), sem("y_v")
    over = {n: sem(f"over_{n}") for n in (
        "shift", "w", "oh", "idxp", "idx", "gat", "xgTp", "xgTs", "xgTv", "gu", "silu", "h", "hTp", "hT", "dn", "ys", "yv", "sc")}
    rows_loaded = [[sem(f"rows_loaded{i}_{b}") for b in range(TB)] for i in range(2)]
    summed = sem("summed")
    root2 = sem("root2")
    stored = sem("stored")

    def fill_s(pe, f):
        n = NO_S[f]
        if n >= RING:
            pe.wait_ge(s_emptied, n - RING + 1)
        return bank[n % RING]

    def fill_v(pe, f):
        n = NO_V[f]
        if n >= RING:
            pe.wait_ge(v_emptied, n - RING + 1)
        return bank[RING + n % RING]

    def full_s(act, f):
        act.wait_ge(s_filled, NO_S[f] + 1)
        return bank[NO_S[f] % RING]

    def full_v(dve, f):
        dve.wait_ge(v_filled, NO_V[f] + 1)
        return bank[RING + NO_V[f] % RING]

    def emptied_s(eng, f):
        eng.wait_ge(s_emptied, NO_S[f] + 1)

    def emptied_v(eng, f):
        eng.wait_ge(v_emptied, NO_V[f] + 1)

    def wait_dma(eng, name, n=1):
        eng.wait_ge(loaded[name], 16 * n)

    NORMED = 2 + 1 + 2 * TB
    def scores_until(q, h):
        return QBS.index(q) * (NI + 1) + h + 1
    def chosen_after(r, phase, n):
        return (2 * r + phase) * len(QBS) + n + 1
    CONV = 4
    UNIT = 4 + 1 + 1 + 4
    units = [(q, g) for q in range(TB) for g in range(2)]

    def att_steps(i, n):
        if n <= 5:
            return 5 * (i + 1) + (UNIT - 5) * max(i - 1, 0) - 5 + n
        return 5 * min(i + 2, len(units)) + (UNIT - 5) * i + n - 5

    LN = 2 + 1 + 1 + 1 + 2
    def weights(slot):
        return slot[:, 0:4096].rearrange("p (g k f) -> p g k f", g=2, k=DK), slot[:, 4096:6144].rearrange("p (k n) -> p k n", k=2)
    sh_gu, sh_d = weights(sh_w)
    Wgu, Wd = zip(*[weights(w) for w in W])
    w_rows = lambda ap: ap.rearrange("(p k) n -> p k n", p=P)

    FINAL = 1 + LN

    TAKEN_STEP = 1 + G + 1 + 1 + 1 + 1 + 1 + 1 + 1 + 1 + 1 + 1 + 1 + 1
    ROUTE = TAKEN_STEP + 1 + 3 + 3 + 5

    def slots4(b):
        return b[:, :].rearrange("p (k c) -> p k c", k=4)[:, :, 0:CAP]

    def slot_weight(buf):
        return w_slot[0:CAP, buf:buf + 1]

    def y_free(e, n):
        return (e - (n % 2)) * 8

    def run_experts(eng, step):
        for e in range(AHEAD):
            step(e, e, first=e == 0)
        with eng.Fori(0, (E - 2 * AHEAD) // UNROLL) as i:
            for n in range(AHEAD, AHEAD + UNROLL):
                step(i * UNROLL + n, n)
        for e in range(E - AHEAD, E):
            step(e, e % UNROLL, last=e == E - 1)

    block = ctx.enter_context(nc.Block())

    @block.sync
    def _(sp):
        x_rows = a["x"][0].rearrange("(b p) d -> p b d", p=P)
        win = w_rows(a["w_in"][0])
        for b in range(TB):
            if b == 2:
                sp.dma_start(w_in[:, :, 0:TOKEN_COLS], win[:, :, 0:TOKEN_COLS]).then_inc(loaded["w_tok"], 16)
            sp.dma_start(X[:, b, :], x_rows[:, b, :]).then_inc(loaded[f"x{b}"], 16)
        sp.dma_start(mem_sb[:, :, :], a["mem"][0].rearrange("(b p) d -> p b d", p=P)).then_inc(loaded["mem"], 16)
        sp.dma_start(wmk[:, :, :], w_rows(a["w_mem_k"][0])).then_inc(loaded["wmk"], 16)
        sp.dma_start(wmv[:, :, :], w_rows(a["w_mem_v"][0])).then_inc(loaded["wmv"], 16)
        for k in range(0, DK, 2):
            sp.dma_start(w_in[:, k:k + 2, TOKEN_COLS:], win[:, k:k + 2, TOKEN_COLS:]).then_inc(loaded["w_chan"], 16)
        sp.wait_ge(s_filled, NO_S["gb", 1] + 1)
        sp.dma_start(w_out[:, :, :], a["w_out"][0].rearrange("(k p) n -> p k n", p=P)).then_inc(loaded["w_out"], 16)
        for name, dst, src in (("g1", g1, a["ln1_g"]), ("b1", b1, a["ln1_b"])):
            sp.dma_start(dst[:, :], src[0].partition_broadcast(P)).then_inc(loaded[name], 16)
        sp.dma_start(w_rt[:, :, :], w_rows(a["w_router"][0])).then_inc(loaded["rt"], 16)
        sp.wait_ge(s_filled, NO_S["ol", TB - 1, 1] + 1)
        sp.dma_start(sh_gu[:, 0, :, :], w_rows(a["w_s_gate"][0])).then_inc(loaded["sh"], 16)
        sp.dma_start(sh_gu[:, 1, :, :], w_rows(a["w_s_up"][0])).then_inc(loaded["sh"], 16)
        sp.dma_start(sh_d, w_rows(a["w_s_down"][0])).then_inc(loaded["sh"], 16)
        sp.dma_start(rb[:, :], a["router_bias"][0].partition_broadcast(P)).then_inc(loaded["rb"], 16)

        def row(t, e):
            return t[0][bass.ds(e, 1)].rearrange("e r n -> (e r) n")

        def load_e(e, s, done):
            sp.dma_start(Wgu[s][:, 0, :, :], w_rows(row(a["w_e_gate"], e))).then_inc(done, 16)
            sp.dma_start(Wgu[s][:, 1, :, :], w_rows(row(a["w_e_up"], e))).then_inc(done, 16)
            sp.dma_start(Wd[s], w_rows(row(a["w_e_down"], e))).then_inc(done, 16)

        sp.wait_ge(s_filled, NO_S["ya", 3] + 1)
        load_e(0, 2, w_loaded[2])
        load_e(1, 3, w_loaded[3])
        x1_rows = x1_dram.rearrange("(b p) d -> p b d", p=P)
        for b in range(TB):
            sp.wait_ge(ln1, LN * (b + 1))
            sp.dma_start(x1_rows[:, b, :], X[:, b, :]).then_inc(x1_stored, 16)
        sp.wait_ge(s_filled, NO_S["rt", TB - 1] + 1)
        load_e(2, 0, w_loaded[0])
        load_e(3, 1, w_loaded[1])
        sp.wait_ge(v_filled, NO_V["yd", TB - 1, 1] + 1)
        for name, dst, src in (("g2", g2, a["ln2_g"]), ("b2", b2, a["ln2_b"])):
            sp.dma_start(dst[:, :], src[0].partition_broadcast(P)).then_inc(loaded[name], 16)
        with sp.Fori(1, E // SLOTS) as i:
            for n in range(SLOTS):
                sp.wait_ge(down_summed, (i * SLOTS + (n + 1 - SLOTS)) * 2)
                load_e(i * SLOTS + n, (n + 2) % SLOTS, w_loaded[(n + 2) % SLOTS])
        def load_rows(i):
            for b in range(TB):
                sp.dma_start(yr[i][:, b, :], y_dram[i][b * P:(b + 1) * P, :]).then_inc(rows_loaded[i][b], 16)

        sp.wait_ge(scattered[0], 16 * (E // 2))
        load_rows(0)
        sp.wait_ge(scattered[1], 16 * (E // 2))
        sp.wait_ge(over["shift"], 1)
        most = sp.value_load(cnt_i[0:1, 0:1], min_val=0, max_val=T)
        with sp.If(most > CAP):
            with sp.Fori(1, ROUNDS) as r:
                with sp.Fori(0, E) as e:
                    n = (r - 1) * E + e
                    sp.wait_ge(over["oh"], n + 1)
                    load_e(e, 0, over["w"])
            sp.wait_ge(over["sc"], 16 * (ROUNDS - 1) * E)
        load_rows(1)
        out_rows = out[0].rearrange("(b p) d -> p b d", p=P)
        for b in range(TB):
            sp.wait_ge(summed, TB + FINAL * (b + 1))
            sp.dma_start(out_rows[:, b, :], sh_acc[:, b, :]).then_inc(stored, 16)
        sp.wait_ge(stored, 16 * TB)

    @block.gpsimd
    def _(pool):
        pool.memset(ident[:, :], 0.0).then_inc(constants, 1)
        pool.memset(causal[:, :], 0.0).then_inc(constants, 1)
        pool.wait_ge(constants, 2)
        pool.affine_select(out=ident[:, :], in_=ident[:, :], compare_op=ALU.not_equal, fill=1.0,
                           base=0, pattern=[[-1, P]], channel_multiplier=1).then_inc(constants, 1)
        pool.affine_select(out=causal[:, :], in_=causal[:, :], compare_op=ALU.is_ge, fill=NEG,
                           base=0, pattern=[[-1, P]], channel_multiplier=1).then_inc(constants, 1)
        emptied_v(pool, ("bias", 1))
        pool.dma_start(bias_dram, rv[0:H, :]).then_inc(bias_stored, 16)
        pool.wait_ge(bias_stored, 16)
        skewed = bass.AP(bias_dram.tensor, 0, [[1, P], [SKEW, H], [1, T]])
        pool.dma_start(B[:, :, :], skewed).then_inc(loaded["bias"], 16)
        pool.memset(zeros[:, :], 0.0).then_inc(constants, 1)
        pool.wait_ge(constants, 5)
        wait_dma(pool, "w_chan", DK // 2)
        for i in range(2):
            for b in range(TB):
                pool.dma_start(y_dram[i][b * P:(b + 1) * P, :].rearrange("p (j c) -> p j c", j=4),
                               zeros[:, :].unsqueeze(1).to_broadcast([P, 4, 256])).then_inc(y_cleared, 16)
        pool.wait_ge(s_filled, NO_S["ol", TB - 1, 1] + 1)
        pool.memset(ones[:, :], 1.0).then_inc(tables, 1)
        pool.memset(tri[:, :], 1.0).then_inc(tables, 1)
        pool.wait_ge(tables, 2)
        pool.affine_select(out=tri[:, :], in_=tri[:, :], compare_op=ALU.is_gt, fill=0.0,
                           base=0, pattern=[[1, P]], channel_multiplier=-1).then_inc(tables, 1)
        pool.iota(iota_c[:, :], [[1, CAP]], base=0, channel_multiplier=0, allow_small_or_imprecise_dtypes=True).then_inc(tables, 1)
        pool.iota(tok[:, :], [[P, TB]], base=0, channel_multiplier=1, allow_small_or_imprecise_dtypes=True).then_inc(tables, 1)
        pool.iota(giota[:, :], [[1, G]], base=0, channel_multiplier=0, allow_small_or_imprecise_dtypes=True).then_inc(tables, 1)
        pool.wait_ge(v_filled, NO_V["gu", TB - 1] + 1)
        for i in range(2):
            pool.memset(xg[i][:, :], 0.0).then_inc(xg_clear, 1)
        pool.wait_ge(xg_clear, 2)
        pool.wait_ge(x1_stored, 16 * TB)

        last_token = pool.to_reg(T - 1)

        def gather(buf, ibuf, done):
            pool.sem_inc(pool_turns, 1)
            pool.indirect_dma_start(out=xg[buf][0:CAP, :], out_offset=None, in_=x1_dram[:, :],
                                    in_offset=bass.IndirectOffsetOnAxis(ap=idx_u[0:CAP, ibuf:ibuf + 1], axis=0),
                                    bounds_check=last_token, oob_is_err=False).then_inc(done, 16)

        def scatter(buf, ibuf, done):
            pool.sem_inc(pool_turns, 1)
            pool.indirect_dma_start(out=y_dram[buf][:, :], out_offset=bass.IndirectOffsetOnAxis(ap=idx_u[0:CAP, ibuf:ibuf + 1], axis=0),
                                    in_=y[buf][0:CAP, :], in_offset=None, bounds_check=last_token, oob_is_err=False,
                                    compute_op=ALU.add).then_inc(done, 16)

        def gather_e(e, n):
            if isinstance(e, int) and e < AHEAD:
                emptied_v(pool, ("slots",))
            else:
                pool.wait_ge(idx_made, (e - AHEAD + 1) * 2)
                pool.wait_ge(xgT_summed, e * 2 - 6)
            gather(n % 4, n % UNROLL, gathered[n % 4])

        def scatter_e(e, n, first=False):
            pool.wait_ge(y_s, e + 1)
            pool.wait_ge(y_v, e + 1)
            if not first:
                pool.wait_ge(scattered[n % 2], y_free(e, n))
            scatter(n % 2, n % UNROLL, scattered[n % 2])

        pool.wait_ge(y_cleared, 2 * TB * 16)
        for e in range(AHEAD):
            if e == 2:
                pool.wait_ge(v_filled, NO_V["yd", TB - 1, 1] + 1)
                for i in (2, 3):
                    pool.memset(xg[i][:, :], 0.0).then_inc(xg_clear, 1)
                pool.wait_ge(xg_clear, 4)
            gather_e(e, e)
        for e in range(AHEAD):
            gather_e(e + AHEAD, e + AHEAD)
            scatter_e(e, e, first=e < 2)
        with pool.Fori(0, (E - 2 * AHEAD) // UNROLL) as i:
            for n in range(AHEAD, AHEAD + UNROLL):
                gather_e(i * UNROLL + (n + AHEAD), n + AHEAD)
                scatter_e(i * UNROLL + n, n)
        for e in range(E - AHEAD, E):
            scatter_e(e, e)
        for i in range(2):
            pool.wait_ge(scattered[i], 16 * (E // 2))
        pool.wait_ge(over["shift"], 1)
        most = pool.value_load(cnt_i[0:1, 0:1], min_val=0, max_val=T)
        with pool.If(most > CAP):
            with pool.Fori(0, (ROUNDS - 1) * E) as n:
                pool.wait_ge(over["idx"], n * 2 + 2)
                gather(0, 0, over["gat"])
                pool.wait_ge(over["ys"], n + 1)
                pool.wait_ge(over["yv"], n + 1)
                scatter(1, 0, over["sc"])
                pool.wait_ge(over["sc"], n * 16 + 16)

    @block.scalar
    def _(act):
        def load(dst, src, name):
            act.dma_start(dst, src).then_inc(loaded[name], 16)

        load(onehot[0:BUCKETS, :], a["buckets"], "bucket")
        load(rel[0:BUCKETS, :], a["rel_bias"], "rel")
        load(w_uk[:, :], a["w_uk"][0].rearrange("c h d -> c (h d)"), "uk")
        load(gq[:, :], a["q_norm_g"][0].partition_broadcast(P), "gq")
        load(gkv[:, :], a["kv_norm_g"][0].partition_broadcast(P), "gkv")
        load(w_qi[:, :, :], a["w_qidx"][0].rearrange("(k p) h d -> p k (h d)", p=P), "qi")
        load(w_uq[:, :, :], a["w_uq"][0].rearrange("(k p) h d -> p k (h d)", p=P), "uq")
        load(w_uv[:, :], a["w_uv"][0].rearrange("c h d -> c (h d)"), "uv")
        for c in range(2):
            for j in range(3):
                load(cw[:, c, j:j + 1], a["conv_w"][0][j:j + 1, c * P:(c + 1) * P].rearrange("o p -> p o"), "cw")

        def empty(f, dst, scale=1.0, view=None):
            b = full_s(act, f)
            act.activation(dst, view(b) if view else b[:, :], ACT.Copy, scale=scale).then_inc(s_emptied, 1)

        four = lambda b: b[:, :].rearrange("p (k t) -> p k t", k=4)
        def x_half(b):
            empty(("xT", b, 0), xT[:, 0:4, b * P:(b + 1) * P], view=four)

        def mem_half(b):
            empty(("memT", b, 0), memT[:, 0:4, b * P:(b + 1) * P], view=four)

        def sum_squares(b):
            emptied_v(act, ("proj", b))
            for k, (lo, n) in enumerate(((0, QR), (QR, KVR))):
                if b or k:
                    act.wait_ge(squares, 2 * b + k)
                else:
                    emptied_v(act, ("proj", 0))
                act.activation(square[:, 0:n], proj[:, b, lo:lo + n], ACT.Square,
                               accum_out=ss[:, k, b:b + 1]).then_inc(squares, 1)

        x_half(0)
        x_half(1)
        x_half(2)
        sum_squares(0)
        x_half(3)
        sum_squares(1)
        mem_half(0)
        sum_squares(2)
        mem_half(1)
        sum_squares(3)
        act.wait_ge(normed, 2)
        act.activation(rms[:, :, :], rms[:, :, :], ACT.Sqrt).then_inc(squares, 1)
        for m in range(2):
            empty(("kmT", m), kmT[:, m, :], view=lambda b: b[:, 0:M])
        act.wait_ge(normed, NORMED)
        empty(("ukT",), ukT[:, :, :], view=four)
        for b in range(TB):
            empty(("cT", b), latT[:, :, b * P:(b + 1) * P], view=four)
        for m in range(4):
            empty(("qiT", m), qiT[:, m, :])
        for n, (q, h) in enumerate((q, h) for q in QBS for h in range(NI)):
            w = (q + 1) * P
            b = full_s(act, ("dot", q, h))
            if n >= 4:
                q0, h0 = QBS[(n - 4) // NI], (n - 4) % NI
                act.wait_ge(scored, scores_until(q0, h0))
            act.activation(relu[:, n % 4, 0:w], b[:, 0:w], ACT.Relu).then_inc(s_emptied, 1)
        for b in range(MB):
            empty(("vm", b), vm[:, b, :], view=lambda b: b[:, 0:MH * HD])
        for m in range(4):
            empty(("qT", m), qT[:, m, :])
        for m in range(2):
            empty(("qm", m), qmT[:, m, :], scale=HD ** -0.5)
        for b in range(TB):
            for j in range(2):
                empty(("ml", b, j), lm[:, b, 2 * j:2 * j + 2, :], view=lambda b: b[:, :].rearrange("p (i m) -> p i m", i=2))

        def mem_exps(b):
            act.wait_ge(mem_soft, 2 * (b + 1))
            for i in range(MH):
                act.activation(lm[:, b, i, :], lm[:, b, i, :], ACT.Exp, bias=mmax[:, b, i:i + 1],
                               accum_out=msum[:, b, i:i + 1]).then_inc(mem_exp, 1)

        for c in range(2):
            empty(("gc", c), gcT[:, c, :])
            empty(("gb", c), gbT[:, c, :])
            if c == 0:
                for b in range(TB):
                    mem_exps(b)
        for h in range(H):
            empty(("ql", h), qlT[:, h, :], scale=HD ** -0.5)

        def mem_outputs():
            for b in range(TB):
                for m in range(MB):
                    empty(("pmT", b, m), pmT[:, m, :, b * P:(b + 1) * P], view=four)
            act.wait_ge(scored, scores_until(QBS[-1], NI - 1))
            for j in range(2):
                empty(("yc", j), mixT[:, 6 + j, :])

        def att_exps(i):
            q, g = units[i]
            w = (q + 1) * P
            act.wait_ge(soft, att_steps(i, 5))
            for h in range(4):
                act.activation(lg[i % 3][:, h, 0:w], lg[i % 3][:, h, 0:w], ACT.Exp, bias=amax[:, i, h:h + 1],
                               accum_out=asum[:, i, h:h + 1]).then_inc(att_exp, 1)

        def latent_out(q, g):
            empty(("ol", q, g), olT[:, 4 * g:4 * g + 4, q * P:(q + 1) * P], view=four)

        mem_outputs()
        att_exps(0)
        for i, (q, g) in enumerate(units):
            if i + 1 < len(units):
                att_exps(i + 1)
            if i == 0:
                act.wait_ge(conv, 2 * CONV)
            for s in range(q + 1):
                if i >= 2:
                    act.wait_ge(s_filled, NO_S[("ol", *units[i - 2])] + 1)
                empty(("pT", q, g, s), pT[i % 2][:, s, :])
            if i:
                latent_out(*units[i - 1])
        latent_out(*units[-1])
        for m in range(4):
            empty(("ya", m), mixT[:, m, :])
        def ln_root(b):
            act.wait_ge(ln1, LN * b + 4)
            act.activation(rstd[:, b:b + 1], rstd[:, b:b + 1], ACT.Sqrt).then_inc(root1, 1)

        def scores_of(b):
            empty(("x1T", b, 0), x1T[:, 0:4, b * P:(b + 1) * P], view=four)
            bk = full_s(act, ("rt", b))
            act.activation(sg_r[:, b, :], bk[:, 0:E], ACT.Sigmoid).then_inc(s_emptied, 1)

        def shared_silu(b):
            act.wait_ge(v_filled, NO_V["gu", b] + 1)
            if b:
                emptied_v(act, ("gu", b - 1))
            act.activation(sh_sg[:, :], bank[RING + NO_V["gu", b] % RING][:, 0:FE], ACT.Silu).then_inc(sh_silu, 1)

        def shared_hT(b):
            bk = full_s(act, ("shT", b))
            if b >= 2:
                act.wait_ge(v_filled, NO_V["yd", b - 2, 1] + 1)
            act.activation(sh_hT[:, b % 2, :, :], bk[:, 0:2 * P].rearrange("p (k t) -> p k t", k=2), ACT.Copy).then_inc(s_emptied, 1)

        for b in range(TB):
            ln_root(b)
            if b + 1 < TB:
                scores_of(b)
        shared_silu(0)
        shared_silu(1)
        scores_of(TB - 1)
        shared_hT(0)
        shared_silu(2)
        shared_hT(1)
        shared_silu(3)
        shared_hT(2)
        shared_hT(3)

        def finish_y(e, n, first=False):
            act.wait_ge(down_summed, e * 2 + 1)
            if not first:
                act.wait_ge(scattered[n % 2], y_free(e, n))
            act.activation(y[n % 2][0:CAP, 0:512], bank[5][0:CAP, :], ACT.Copy, scale=slot_weight(n % UNROLL)).then_inc(y_s, 1)

        def transpose_x(e, n):
            act.wait_ge(xgT_summed, e * 2 + 1)
            act.activation(xgT[n % 2][:, 0:4, :], slots4(bank[2]), ACT.Copy).then_inc(xgT_s, 1)

        def expert(e, n, first=False, last=False):
            act.wait_ge(w_loaded[(n + 2) % SLOTS], (e - n % SLOTS) * 12 + 48)
            if isinstance(e, int) and e < 2:
                emptied_v(act, ("yd", TB - 1, 1))
            else:
                act.wait_ge(down_summed, e * 2 - 2)
            act.activation(wd_hi[n % 2][:, :, :], Wd[(n + 2) % SLOTS], ACT.Copy).then_inc(hi_made, 1)
            act.wait_ge(gu_summed, e + 1)
            if not first:
                act.wait_ge(h_made, e)
            act.activation(sg[0:CAP, :], bank[0][0:CAP, 0:FE], ACT.Silu).then_inc(silu_made, 1)
            if not last:
                transpose_x(e + 1, n + 1)
            if not first:
                finish_y(e - 1, n - 1, first=isinstance(e, int) and e - 1 < 2)
            act.wait_ge(hT_summed, e + 1)
            if first:
                act.wait_ge(hT_padded, 2)
            else:
                act.wait_ge(down_summed, e * 2)
            act.activation(hT_hi[:, :, 0:CAP], slots4(bank[4])[:, 0:2, :], ACT.Copy).then_inc(hT_hi_made, 1)

        transpose_x(0, 0)
        run_experts(act, expert)
        finish_y(E - 1, E - 1)
        act.wait_ge(over["shift"], 1)
        most = act.value_load(cnt_i[0:1, 0:1], min_val=0, max_val=T)
        with act.If(most > CAP):
            with act.Fori(0, (ROUNDS - 1) * E) as n:
                act.wait_ge(over["xgTp"], n * 2 + 1)
                act.activation(xgT[0][:, 0:4, :], slots4(bank[2]), ACT.Copy).then_inc(over["xgTs"], 1)
                act.wait_ge(over["gu"], n + 1)
                act.activation(sg[0:CAP, :], bank[0][0:CAP, 0:FE], ACT.Silu).then_inc(over["silu"], 1)
                act.wait_ge(over["hTp"], n + 1)
                act.activation(hT[:, :, :], slots4(bank[4])[:, 0:2, :], ACT.Copy).then_inc(over["hT"], 1)
                act.wait_ge(over["dn"], n * 2 + 1)
                act.activation(y[1][0:CAP, 0:512], bank[5][0:CAP, :], ACT.Copy, scale=slot_weight(0)).then_inc(over["ys"], 1)
        for b in range(TB):
            act.wait_ge(summed, TB + FINAL * b + 1 + 4)
            act.activation(rstd2[:, b:b + 1], rstd2[:, b:b + 1], ACT.Sqrt).then_inc(root2, 1)

    @block.vector
    def _(dve):
        def empty(f, dst, view=None):
            b = full_v(dve, f)
            dve.tensor_copy(dst, view(b) if view else b[:, :]).then_inc(v_emptied, 1)

        def layer_norm(src, dst, stats, mean_var, r, gain, bias, done, start, root, roots):
            for c in range(2):
                dve.bn_stats(stats[:, c, :], src[:, c * 512:(c + 1) * 512]).then_inc(done, 1)
            dve.wait_ge(done, start + 2)
            dve.bn_aggr(mean_var, stats).then_inc(done, 1)
            dve.wait_ge(done, start + 3)
            dve.tensor_scalar(r, mean_var[:, 1:2], LN_EPS, None, ALU.add).then_inc(done, 1)
            dve.wait_ge(root, roots)
            dve.reciprocal(r, r).then_inc(done, 1)
            dve.wait_ge(done, start + 5)
            dve.scalar_tensor_tensor(src, src, mean_var[:, 0:1], gain, ALU.subtract, ALU.mult).then_inc(done, 1)
            dve.wait_ge(done, start + 6)
            dve.scalar_tensor_tensor(dst, src, r, bias, ALU.mult, ALU.add).then_inc(done, 1)

        empty(("bias", 0), rv[0:H, 0:512], view=lambda b: b[0:H, :])
        empty(("bias", 1), rv[0:H, 512:SKEW], view=lambda b: b[0:H, 0:SKEW - 512])
        four = lambda b: b[:, :].rearrange("p (k t) -> p k t", k=4)
        def x_half(b):
            empty(("xT", b, 1), xT[:, 4:8, b * P:(b + 1) * P], view=four)

        def mem_half(b):
            empty(("memT", b, 1), memT[:, 4:8, b * P:(b + 1) * P], view=four)

        def projected(b):
            bk = full_v(dve, ("proj", b))
            dve.tensor_copy(proj[:, b, :], bk[:, 0:QR + KVR])
            dve.tensor_copy(kk[:, b, :, :], bk[:, QR + KVR:QR + KVR + IDX].unsqueeze(1).to_broadcast([P, 2, IDX]))
            dve.tensor_scalar(iw[:, b, :], bk[:, QR + KVR + IDX:TOKEN_COLS], NI ** -0.5 * IDX ** -0.5, None,
                              ALU.mult).then_inc(v_emptied, 1)

        x_half(0)
        x_half(1)
        projected(0)
        x_half(2)
        projected(1)
        x_half(3)
        projected(2)
        mem_half(0)
        projected(3)
        mem_half(1)
        dve.wait_ge(squares, 2 * TB)
        for k, n in enumerate((QR, KVR)):
            dve.tensor_scalar(rms[:, k, :], ss[:, k, :], 1.0 / n, RMS_EPS, ALU.mult, ALU.add).then_inc(normed, 1)
        dve.wait_ge(squares, 2 * TB + 1)
        dve.reciprocal(rms[:, :, :], rms[:, :, :]).then_inc(normed, 1)
        dve.wait_ge(normed, 3)
        wait_dma(dve, "gq")
        wait_dma(dve, "gkv")
        for b in range(TB):
            dve.scalar_tensor_tensor(proj[:, b, 0:QR], proj[:, b, 0:QR], rms[:, 0, b:b + 1], gq[:, :],
                                     ALU.mult, ALU.mult).then_inc(normed, 1)
            dve.scalar_tensor_tensor(ckvn[:, b, :], proj[:, b, QR:QR + KVR], rms[:, 1, b:b + 1], gkv[:, :],
                                     ALU.mult, ALU.mult).then_inc(normed, 1)
        for q in QBS:
            w = (q + 1) * P
            sq = sel[:, q - 1, 0:w]
            for h in range(NI):
                emptied_s(dve, ("dot", q, h))
                r = relu[:, NO_S["dot", q, h] - NO_S["dot", QBS[0], 0] & 3, 0:w]
                if h == 0:
                    dve.tensor_scalar(sq, r, iw[:, q, 0:1], None, ALU.mult).then_inc(scored, 1)
                else:
                    dve.wait_ge(scored, scores_until(q, h - 1))
                    dve.scalar_tensor_tensor(sq, r, iw[:, q, h:h + 1], sq, ALU.mult, ALU.add).then_inc(scored, 1)
            dve.wait_ge(scored, scores_until(q, NI - 1))
            dve.wait_ge(constants, 4)
            dve.tensor_tensor(sel[:, q - 1, q * P:w], sel[:, q - 1, q * P:w], causal[:, :], ALU.add).then_inc(scored, 1)
        dve.wait_ge(scored, len(QBS) * (NI + 1))
        for r in range(TOPK // 8):
            for n, q in enumerate(QBS):
                if r:
                    dve.wait_ge(chosen, chosen_after(r - 1, 1, n))
                dve.max(top8[:, n, :], sel[:, q - 1, 0:(q + 1) * P]).then_inc(chosen, 1)
            for n, q in enumerate(QBS):
                sq = sel[:, q - 1, 0:(q + 1) * P]
                dve.wait_ge(chosen, chosen_after(r, 0, n))
                dve.match_replace(sq, top8[:, n, :], sq, TAKEN).then_inc(chosen, 1)
        for n, q in enumerate(QBS):
            sq = sel[:, q - 1, 0:(q + 1) * P]
            dve.wait_ge(chosen, chosen_after(TOPK // 8 - 1, 1, n))
            dve.tensor_scalar(sq, sq, MIDWAY, NEG, ALU.is_ge, ALU.mult).then_inc(chosen, 1)

        def mem_max(b):
            emptied_s(dve, ("ml", b, 1))
            dve.reduce_max(mmax[:, b, :], lm[:, b, :, :], AX.X).then_inc(mem_soft, 1)
            dve.wait_ge(mem_soft, 2 * b + 1)
            dve.tensor_scalar(mmax[:, b, :], mmax[:, b, :], -1.0, None, ALU.mult).then_inc(mem_soft, 1)

        def mem_norm(b):
            dve.wait_ge(mem_exp, MH * (b + 1))
            dve.reciprocal(msum[:, b, :], msum[:, b, :]).then_inc(mem_soft, 1)
            dve.wait_ge(mem_soft, 2 * TB + 2 * b + 1)
            dve.tensor_tensor(lm[:, b, :, :], lm[:, b, :, :], msum[:, b, :].unsqueeze(2).to_broadcast([P, MH, M]),
                              ALU.mult).then_inc(mem_soft, 1)

        def convolution(c):
            dve.memset(u[:, c, 0:2], 0.0)
            emptied_s(dve, ("gc", c))
            bk = full_v(dve, ("hc", c))
            dve.tensor_tensor(u[:, c, 2:], gcT[:, c, :], bk[:, :], ALU.mult).then_inc(v_emptied, 1)
            emptied_v(dve, ("hc", c))
            dve.tensor_scalar(cv[:, c, :], u[:, c, 0:T], cw[:, c, 0:1], None, ALU.mult).then_inc(conv, 1)
            for j in (1, 2):
                dve.wait_ge(conv, CONV * c + j)
                dve.scalar_tensor_tensor(cv[:, c, :], u[:, c, j:j + T], cw[:, c, j:j + 1], cv[:, c, :],
                                         ALU.mult, ALU.add).then_inc(conv, 1)
            dve.wait_ge(conv, CONV * c + 3)
            emptied_s(dve, ("gb", c))
            dve.tensor_tensor(mixT[:, 4 + c, :], cv[:, c, :], gbT[:, c, :], ALU.mult).then_inc(conv, 1)

        for b in range(TB):
            mem_max(b)
        wait_dma(dve, "cw", 6)
        dve.wait_ge(bias_stored, 16)
        convolution(0)
        for b in range(TB):
            mem_norm(b)
        convolution(1)

        wait_dma(dve, "bias")

        def bias_of(h, w):
            return B[:, h, w - 1::-1]

        def att_max(i):
            q, g = units[i]
            w = (q + 1) * P
            mask = causal[:, :] if q == 0 else sel[:, q - 1, 0:w]
            if i == 2:
                dve.wait_ge(s_filled, NO_S["yc", 1] + 1)
            if i >= 3:
                dve.wait_ge(s_filled, NO_S[("pT", *units[i - 3], units[i - 3][0])] + 1)
            for h in range(4):
                bk = full_v(dve, ("lg", q, g, h))
                dve.tensor_tensor(lg[i % 3][:, h, 0:w], bias_of(4 * g + h, w), bk[:, 0:w], ALU.add).then_inc(v_emptied, 1)
            for h in range(4):
                emptied_v(dve, ("lg", q, g, h))
                dve.tensor_tensor_reduce(out=lg[i % 3][:, h, 0:w], in0=lg[i % 3][:, h, 0:w], in1=mask, scale=1.0,
                                         scalar=-3.4e38, op0=ALU.add, op1=ALU.max,
                                         accum_out=amax[:, i, h:h + 1]).then_inc(soft, 1)
            dve.wait_ge(soft, att_steps(i, 4))
            dve.tensor_scalar(amax[:, i, :], amax[:, i, :], -1.0, None, ALU.mult).then_inc(soft, 1)

        def att_norm(i):
            q, g = units[i]
            w = (q + 1) * P
            dve.wait_ge(att_exp, 4 * (i + 1))
            dve.reciprocal(asum[:, i, :], asum[:, i, :]).then_inc(soft, 1)
            dve.wait_ge(soft, att_steps(i, 6))
            for h in range(4):
                dve.tensor_scalar(lg[i % 3][:, h, 0:w], lg[i % 3][:, h, 0:w], asum[:, i, h:h + 1], None,
                                  ALU.mult).then_inc(soft, 1)

        att_max(0)
        for i in range(len(units)):
            if i + 1 < len(units):
                att_max(i + 1)
            att_norm(i)
        wait_dma(dve, "g1")
        wait_dma(dve, "b1")
        def residual(b, j):
            bk = full_v(dve, ("mo", b, j))
            xs = X[:, b, j * 512:(j + 1) * 512]
            dve.scalar_tensor_tensor(xs, xs, ALPHA, bk[:, :], ALU.mult, ALU.add).then_inc(v_emptied, 1)

        def first_norm(b):
            emptied_v(dve, ("mo", b, 1))
            layer_norm(X[:, b, :], X[:, b, :], bn[:, b, :, :], mv[:, b, :], rstd[:, b:b + 1], g1[:, :], b1[:, :],
                       ln1, LN * b, root1, b + 1)

        def x1_half(b):
            empty(("x1T", b, 1), x1T[:, 4:8, b * P:(b + 1) * P], view=four)

        steps = [0]

        def step(ins):
            ins.then_inc(routed, 1)
            steps[0] += 1

        def after():
            dve.wait_ge(routed, steps[0])

        by_group = lambda t, b: t[:, b, :].rearrange("p (g j) -> p g j", g=G)

        def route(b):
            emptied_s(dve, ("rt", b))
            step(dve.tensor_tensor(sc[:, b, :], sg_r[:, b, :], rb[:, :], ALU.add))
            after()
            for g in range(G):
                step(dve.max(g8[:, b, g, :], sc[:, b, g * EG:(g + 1) * EG]))
            after()
            step(dve.tensor_tensor(gs[:, b, :], g8[:, b, :, 0], g8[:, b, :, 1], ALU.add))
            after()
            step(dve.max(gtop[:, b, :], gs[:, b, :]))
            after()
            step(dve.max_index(gidx[:, b, :], gtop[:, b, :], gs[:, b, :]))
            after()
            step(dve.tensor_copy(gif[:, b, :], gidx[:, b, :]))
            after()
            step(dve.tensor_tensor(gcmp[:, b, :, :], giota[:, :].unsqueeze(2).to_broadcast([P, G, TOPG]),
                                   gif[:, b, 0:TOPG].unsqueeze(1).to_broadcast([P, G, TOPG]), ALU.is_equal))
            after()
            step(dve.tensor_reduce(gmask[:, b, :], gcmp[:, b, :, :], AX.X, ALU.add))
            after()
            step(dve.tensor_tensor(by_group(cand, b), by_group(sc, b), gmask[:, b, :].unsqueeze(2).to_broadcast([P, G, EG]), ALU.mult))
            after()
            step(dve.tensor_scalar(gmask[:, b, :], gmask[:, b, :], -1.0, -NEG, ALU.add, ALU.mult))
            after()
            step(dve.tensor_tensor(by_group(cand, b), by_group(cand, b), gmask[:, b, :].unsqueeze(2).to_broadcast([P, G, EG]), ALU.add))
            after()
            step(dve.max(etop[:, b, :], cand[:, b, :]))
            after()
            step(dve.match_replace(cand[:, b, :], etop[:, b, :], cand[:, b, :], TAKEN))
            after()
            step(dve.tensor_scalar(took[:, b, :], cand[:, b, :], MIDWAY, None, ALU.is_lt))
            assert steps[0] == ROUTE * b + TAKEN_STEP
            step(dve.tensor_scalar(taken[:, b, :], cand[:, b, :], MIDWAY, None, ALU.is_lt))
            after()
            step(dve.tensor_tensor(wts[:, b, :], sg_r[:, b, :], taken[:, b, :], ALU.mult))
            step(dve.tensor_scalar(tab[:, b, :, 0], taken[:, b, :], 0.0, -FAR, ALU.mult, ALU.add))
            step(dve.tensor_scalar(tab[:, b, :, 1], taken[:, b, :], 0.0, tok[:, b:b + 1], ALU.mult, ALU.add))
            after()
            step(dve.reduce_sum(wsum[:, b:b + 1], wts[:, b, :], AX.X))
            after()
            step(dve.reciprocal(wrec[:, b:b + 1], wsum[:, b:b + 1]))
            after()
            step(dve.tensor_scalar(rest[:, b, :], wts[:, b, :], wrec[:, b:b + 1], 2.5, ALU.mult, ALU.mult))
            after()
            for part in range(3):
                step(dve.tensor_copy(tab[:, b, :, 2 + part], rest[:, b, :]))
                after()
                if part < 2:
                    step(dve.tensor_tensor(rest[:, b, :], rest[:, b, :], tab[:, b, :, 2 + part], ALU.subtract))
                    after()

        def shared_mul(b):
            bk = full_v(dve, ("gu", b))
            dve.wait_ge(sh_silu, b + 1)
            dve.tensor_tensor(sh_h[:, b, :], sh_sg[:, :], bk[:, FE:2 * FE], ALU.mult).then_inc(v_emptied, 1)

        def shared_add(b):
            for j in range(2):
                bk = full_v(dve, ("yd", b, j))
                dve.scalar_tensor_tensor(sh_acc[:, b, j * 512:(j + 1) * 512], X[:, b, j * 512:(j + 1) * 512], ALPHA, bk[:, :],
                                         ALU.mult, ALU.add).then_inc(v_emptied, 1)

        def slots_of(e, dst, done):
            dve.tensor_tensor(dst[:, :, :], iota_c[:, :].unsqueeze(1).to_broadcast([P, TB, CAP]),
                              posm[:, :, bass.ds(e, 1)].to_broadcast([P, TB, CAP]), ALU.is_equal).then_inc(done, 1)

        def weight_of(row, buf):
            return dve.reduce_sum(slot_weight(buf), row[:, 2:COLS], AX.X)

        def index_of(row, buf):
            return dve.tensor_scalar(idx_u[0:CAP, buf:buf + 1], row[:, 1:2], row[:, 0:1], FAR + HALF, ALU.add, ALU.add)

        dve.wait_ge(tables, 6)
        dve.tensor_scalar(tok[:, :], tok[:, :], -float(HALF), None, ALU.add).then_inc(tables, 1)
        dve.wait_ge(tables, 7)
        wait_dma(dve, "g1")
        wait_dma(dve, "b1")
        wait_dma(dve, "rb")
        for b in range(TB):
            residual(b, 0)
            if b:
                x1_half(b - 1)
            if b >= 2:
                route(b - 2)
            residual(b, 1)
            first_norm(b)
        route(TB - 2)
        shared_mul(0)
        shared_mul(1)
        x1_half(TB - 1)
        route(TB - 1)
        shared_mul(2)
        shared_add(0)
        bk = full_v(dve, ("pos",))
        dve.scalar_tensor_tensor(posm[:, :, :], bk[:, 0:TB * E].rearrange("p (b e) -> p b e", b=TB), 1.0, taken[:, :, :],
                                 ALU.add, ALU.mult).then_inc(v_emptied, 1)
        emptied_v(dve, ("pos",))
        step(dve.tensor_scalar(posm[:, :, :], posm[:, :, :], -1.0, None, ALU.add))
        after()
        for e in range(AHEAD):
            slots_of(e, oh[e], oh_made)
        bk = full_v(dve, ("cnt",))
        dve.reduce_max(cnt[:, :], bk[:, 0:E], AX.X).then_inc(v_emptied, 1)
        emptied_v(dve, ("cnt",))
        step(dve.tensor_copy(cnt_i[:, :], cnt[:, :]))
        shared_mul(3)
        bk = full_v(dve, ("slots",))
        for e in range(AHEAD):
            weight_of(bk[0:CAP, COLS * e:COLS * (e + 1)], e)
            last = index_of(bk[0:CAP, COLS * e:COLS * (e + 1)], e)
        last.then_inc(v_emptied, 1)
        for b in range(1, TB):
            shared_add(b)

        def indices(buf, done):
            weight_of(bank[1][0:CAP, 0:COLS], buf).then_inc(done, 1)
            index_of(bank[1][0:CAP, 0:COLS], buf).then_inc(done, 1)

        def finish_y(e, n, first=False):
            dve.wait_ge(down_summed, e * 2 + 2)
            if not first:
                dve.wait_ge(scattered[n % 2], y_free(e, n))
            dve.tensor_scalar(y[n % 2][0:CAP, 512:1024], bank[6][0:CAP, :], slot_weight(n % UNROLL), None, ALU.mult).then_inc(y_v, 1)

        def transpose_x(e, n):
            dve.wait_ge(xgT_summed, e * 2 + 2)
            dve.tensor_copy(xgT[n % 2][:, 4:8, :], slots4(bank[3])).then_inc(xgT_v, 1)

        def make_slots(e, n):
            if not isinstance(e, int) or e >= 2 * AHEAD:
                dve.wait_ge(idx_summed, e - (2 * AHEAD - 1))
            slots_of(e, oh[n % AHEAD], oh_made)

        def make_indices(e, n):
            dve.wait_ge(idx_summed, e - (AHEAD - 1))
            indices(n % UNROLL, idx_made)

        def expert(e, n, first=False, last=False):
            tail = isinstance(e, int) and e >= E - AHEAD
            if not first and not (tail and e + AHEAD - 1 >= E):
                make_indices(e + (AHEAD - 1), n + AHEAD - 1)
            dve.wait_ge(hi_made, e + 1)
            s = (n + 2) % SLOTS
            dve.tensor_tensor(wd_lo[s][:, :, :], Wd[s], wd_hi[n % 2][:, :, :], ALU.subtract).then_inc(lo_made, 1)
            dve.wait_ge(silu_made, e + 1)
            if not first:
                dve.wait_ge(hT_summed, e)
            dve.tensor_tensor(h_sb[0:CAP, :], sg[0:CAP, :], bank[0][0:CAP, FE:2 * FE], ALU.mult).then_inc(h_made, 1)
            if not last:
                transpose_x(e + 1, n + 1)
            if not tail:
                make_slots(e + AHEAD, n + AHEAD)
            if not first:
                finish_y(e - 1, n - 1, first=isinstance(e, int) and e - 1 < 2)
            dve.wait_ge(hT_hi_made, e + 1)
            dve.tensor_tensor(hT_lo[:, :, 0:CAP], slots4(bank[4])[:, 0:2, :], hT_hi[:, :, 0:CAP], ALU.subtract).then_inc(hT_lo_made, 1)

        for part in (hT_hi, hT_lo):
            if CAP < P:
                dve.tensor_copy(part[:, :, CAP:P], zeros[:, 0:2 * (P - CAP)].rearrange("p (k c) -> p k c", k=2)).then_inc(hT_padded, 1)
        transpose_x(0, 0)
        run_experts(dve, expert)
        finish_y(E - 1, E - 1)
        for b in range(TB):
            dve.wait_ge(rows_loaded[0][b], 16)
            dve.tensor_tensor(sh_acc[:, b, :], sh_acc[:, b, :], yr[0][:, b, :], ALU.add).then_inc(summed, 1)
        dve.engine_nop().then_inc(over["shift"], 1)
        most = dve.value_load(cnt_i[0:1, 0:1], min_val=0, max_val=T)
        with dve.If(most > CAP):
            for i in range(2):
                dve.wait_ge(scattered[i], 16 * (E // 2))
            with dve.Fori(1, ROUNDS) as r:
                dve.tensor_scalar(posm[:, :, :], posm[:, :, :], -float(CAP), None, ALU.add).then_inc(over["shift"], 1)
                with dve.Fori(0, E) as e:
                    n = (r - 1) * E + e
                    dve.wait_ge(over["shift"], r + 1)
                    slots_of(e, oh[0], over["oh"])
                    dve.wait_ge(over["idxp"], n + 1)
                    indices(0, over["idx"])
                    dve.wait_ge(over["xgTp"], n * 2 + 2)
                    dve.tensor_copy(xgT[0][:, 4:8, :], slots4(bank[3])).then_inc(over["xgTv"], 1)
                    dve.wait_ge(over["silu"], n + 1)
                    dve.tensor_tensor(h_sb[0:CAP, :], sg[0:CAP, :], bank[0][0:CAP, FE:2 * FE], ALU.mult).then_inc(over["h"], 1)
                    dve.wait_ge(over["dn"], n * 2 + 2)
                    dve.tensor_scalar(y[1][0:CAP, 512:1024], bank[6][0:CAP, :], slot_weight(0), None, ALU.mult).then_inc(over["yv"], 1)
                    dve.wait_ge(over["sc"], n * 16 + 16)
        wait_dma(dve, "g2")
        wait_dma(dve, "b2")
        for b in range(TB):
            dve.wait_ge(rows_loaded[1][b], 16)
            dve.tensor_tensor(sh_acc[:, b, :], sh_acc[:, b, :], yr[1][:, b, :], ALU.add).then_inc(summed, 1)
            dve.wait_ge(summed, TB + FINAL * b + 1)
            layer_norm(sh_acc[:, b, :], sh_acc[:, b, :], bn2[:, b, :, :], mv2[:, b, :], rstd2[:, b:b + 1], g2[:, :], b2[:, :],
                       summed, TB + FINAL * b + 1, root2, b + 1)

    @block.tensor
    def _(pe):
        def mm(dst, lhsT, rhs, start, stop):
            return pe.matmul(dst, lhsT, rhs, start=start, stop=stop)

        def transposes(dst, srcs):
            for i, s in enumerate(srcs):
                last = pe.transpose(dst[:, i * P:i * P + s.shape[0]], s, ident[0:s.shape[0], 0:s.shape[0]])
            return last

        def summed(dst, pairs):
            for i, (l, r) in enumerate(pairs):
                last = mm(dst, l, r, i == 0, i == len(pairs) - 1)
            return last

        wait_dma(pe, "bucket")
        wait_dma(pe, "rel")
        for n, (lo, hi) in enumerate(((0, 512), (512, SKEW))):
            b = fill_v(pe, ("bias", n))
            mm(b[0:H, 0:hi - lo], rel[0:BUCKETS, :], onehot[0:BUCKETS, lo:hi], True, True).then_inc(v_filled, 1)
        pe.wait_ge(constants, 3)
        def turned(name, b, src):
            cols = src.rearrange("p (c k) -> p k c", k=DK)
            transposes(fill_s(pe, (name, b, 0)), [cols[:, k, :] for k in range(4)]).then_inc(s_filled, 1)
            transposes(fill_v(pe, (name, b, 1)), [cols[:, k, :] for k in range(4, 8)]).then_inc(v_filled, 1)

        def x_turned(b):
            wait_dma(pe, f"x{b}")
            turned("xT", b, X[:, b, :])

        def project(b):
            emptied_s(pe, ("xT", b, 0))
            emptied_v(pe, ("xT", b, 1))
            summed(fill_v(pe, ("proj", b))[:, 0:TOKEN_COLS],
                   [(xT[:, k, b * P:(b + 1) * P], w_in[:, k, 0:TOKEN_COLS]) for k in range(DK)]).then_inc(v_filled, 1)

        x_turned(0)
        x_turned(1)
        wait_dma(pe, "w_tok")
        project(0)
        x_turned(2)
        project(1)
        x_turned(3)
        project(2)
        wait_dma(pe, "mem")
        turned("memT", 0, mem_sb[:, 0, :])
        project(3)
        turned("memT", 1, mem_sb[:, 1, :])
        emptied_s(pe, ("memT", MB - 1, 0))
        emptied_v(pe, ("memT", MB - 1, 1))
        wait_dma(pe, "wmk")
        for m in range(2):
            summed(fill_s(pe, ("kmT", m))[:, 0:M],
                   [(wmk[:, k, m * P:(m + 1) * P], memT[:, k, :]) for k in range(DK)]).then_inc(s_filled, 1)
        wait_dma(pe, "uk")
        transposes(fill_s(pe, ("ukT",)), [w_uk[:, m * P:(m + 1) * P] for m in range(4)]).then_inc(s_filled, 1)
        pe.wait_ge(normed, NORMED)
        for b in range(TB):
            transposes(fill_s(pe, ("cT", b)), [proj[:, b, 0:P], proj[:, b, P:2 * P], ckvn[:, b, :],
                                               kk[:, b, :, :].rearrange("p i d -> p (i d)")]).then_inc(s_filled, 1)
        emptied_s(pe, ("cT", TB - 1))
        wait_dma(pe, "qi")
        for m in range(4):
            summed(fill_s(pe, ("qiT", m))[:, :], [(w_qi[:, k, m * P:(m + 1) * P], latT[:, k, :]) for k in range(2)]).then_inc(s_filled, 1)
        for q in QBS:
            w = (q + 1) * P
            for h in range(NI):
                emptied_s(pe, ("qiT", h // 2))
                lo = h % 2 * IDX
                b = fill_s(pe, ("dot", q, h))
                mm(b[:, 0:w], qiT[lo:lo + IDX, h // 2, q * P:(q + 1) * P], latT[lo:lo + IDX, 3, 0:w], True, True).then_inc(s_filled, 1)

        def channels(dst, lo):
            return summed(dst[:, :], [(w_in[:, k, lo:lo + P], xT[:, k, :]) for k in range(DK)])

        wait_dma(pe, "wmv")
        for b in range(MB):
            summed(fill_s(pe, ("vm", b))[:, 0:MH * HD],
                   [(memT[:, k, b * P:(b + 1) * P], wmv[:, k, :]) for k in range(DK)]).then_inc(s_filled, 1)
        wait_dma(pe, "uq")
        for m in range(4):
            summed(fill_s(pe, ("qT", m))[:, :], [(w_uq[:, k, m * P:(m + 1) * P], latT[:, k, :]) for k in range(2)]).then_inc(s_filled, 1)
        wait_dma(pe, "w_chan", DK // 2)
        for m in range(2):
            channels(fill_s(pe, ("qm", m)), TOKEN_COLS + 3 * CC + m * P).then_inc(s_filled, 1)
        emptied_s(pe, ("qm", 1))
        emptied_s(pe, ("vm", MB - 1))
        for b in range(TB):
            for j in range(2):
                bk = fill_s(pe, ("ml", b, j))
                for i in range(2):
                    last = mm(bk[:, i * M:(i + 1) * M], qmT[j * HD:(j + 1) * HD, i, b * P:(b + 1) * P], kmT[j * HD:(j + 1) * HD, i, :], True, True)
                last.then_inc(s_filled, 1)
        for c in range(2):
            channels(fill_s(pe, ("gc", c)), TOKEN_COLS + CC + c * P).then_inc(s_filled, 1)
            channels(fill_v(pe, ("hc", c)), TOKEN_COLS + 2 * CC + c * P).then_inc(v_filled, 1)
            channels(fill_s(pe, ("gb", c)), TOKEN_COLS + c * P).then_inc(s_filled, 1)
        emptied_s(pe, ("qT", 3))
        for h in range(H):
            lo = h % 2 * HD
            mm(fill_s(pe, ("ql", h))[:, :], ukT[lo:lo + HD, h // 2, :], qT[lo:lo + HD, h // 2, :], True, True).then_inc(s_filled, 1)
        emptied_s(pe, ("ql", H - 1))

        def logits(i):
            q, g = units[i]
            w = (q + 1) * P
            for h in range(4):
                mm(fill_v(pe, ("lg", q, g, h))[:, 0:w], qlT[:, 4 * g + h, q * P:(q + 1) * P], latT[:, 2, 0:w], True, True).then_inc(v_filled, 1)

        logits(0)
        for b in range(TB):
            pe.wait_ge(mem_soft, 2 * TB + 2 * (b + 1))
            for m in range(MB):
                transposes(fill_s(pe, ("pmT", b, m)), [lm[:, b, s, m * P:(m + 1) * P] for s in range(MH)]).then_inc(s_filled, 1)
        emptied_s(pe, ("pmT", TB - 1, MB - 1))
        for i in range(2):
            bk = fill_s(pe, ("yc", i))
            for j in range(2):
                h = 2 * i + j
                for m in range(MB):
                    last = mm(bk[j * HD:(j + 1) * HD, :], vm[:, m, h * HD:(h + 1) * HD], pmT[:, m, 2 * j + i, :], m == 0, m == MB - 1)
            last.then_inc(s_filled, 1)
        def latent_out(i):
            q, g = units[i]
            bk = fill_s(pe, ("ol", q, g))
            for s in range(q + 1):
                emptied_s(pe, ("pT", q, g, s))
                last = mm(bk[:, :], ckvn[:, s, :], pT[i % 2][:, s, :], s == 0, s == q)
            last.then_inc(s_filled, 1)

        logits(1)
        for i, (q, g) in enumerate(units):
            if i + 2 < len(units):
                logits(i + 2)
            pe.wait_ge(soft, att_steps(i, UNIT))
            for s in range(q + 1):
                transposes(fill_s(pe, ("pT", q, g, s)), [lg[i % 3][:, h, s * P:(s + 1) * P] for h in range(4)]).then_inc(s_filled, 1)
            if i:
                latent_out(i - 1)
        latent_out(len(units) - 1)
        emptied_s(pe, ("ol", TB - 1, 1))
        for m in range(4):
            bk = fill_s(pe, ("ya", m))
            for j in range(2):
                h = 2 * m + j
                last = mm(bk[j * HD:(j + 1) * HD, :], w_uv[:, h * HD:(h + 1) * HD], olT[:, h, :], True, True)
            last.then_inc(s_filled, 1)
        wait_dma(pe, "w_out")
        emptied_s(pe, ("ya", 3))
        pe.wait_ge(conv, 2 * CONV)
        def output(b, j):
            summed(fill_v(pe, ("mo", b, j))[:, :],
                   [(mixT[:, k, b * P:(b + 1) * P], w_out[:, k, j * 512:(j + 1) * 512]) for k in range(DK)]).then_inc(v_filled, 1)

        def x1_transposed(b):
            pe.wait_ge(ln1, LN * (b + 1))
            turned("x1T", b, X[:, b, :])

        def router_logits(b):
            emptied_s(pe, ("x1T", b, 0))
            emptied_v(pe, ("x1T", b, 1))
            summed(fill_s(pe, ("rt", b))[:, 0:E], [(x1T[:, k, b * P:(b + 1) * P], w_rt[:, k, :]) for k in range(DK)]).then_inc(s_filled, 1)

        def gate_up(dst, xt, w):
            return summed(dst, [(xt[:, k, :], w[:, :, k, :]) for k in range(DK)])

        def shared_up(b):
            gate_up(fill_v(pe, ("gu", b))[:, :], x1T[:, :, b * P:(b + 1) * P], sh_gu).then_inc(v_filled, 1)

        def shared_turned(b):
            emptied_v(pe, ("gu", b))
            hh = sh_h[:, b, :].rearrange("p (c k) -> p k c", k=2)
            transposes(fill_s(pe, ("shT", b)), [hh[:, k, :] for k in range(2)]).then_inc(s_filled, 1)

        def shared_down(b):
            emptied_s(pe, ("shT", b))
            for j in range(2):
                summed(fill_v(pe, ("yd", b, j))[:, :], [(sh_hT[:, b % 2, k, :], sh_d[:, k, j * 512:(j + 1) * 512]) for k in range(2)]).then_inc(v_filled, 1)

        def slot_table(dst, e, buf):
            return summed(dst, [(oh[buf][:, b, :], tab[:, b, bass.ds(e, 1), :].rearrange("p e c -> p (e c)")) for b in range(TB)])

        output(0, 0)
        output(0, 1)
        wait_dma(pe, "rt")
        for b in range(1, TB):
            output(b, 0)
            x1_transposed(b - 1)
            output(b, 1)
            router_logits(b - 1)
        wait_dma(pe, "sh", 3)
        shared_up(0)
        shared_up(1)
        x1_transposed(TB - 1)
        router_logits(TB - 1)
        shared_turned(0)
        shared_up(2)
        shared_down(0)
        pe.wait_ge(routed, ROUTE * (TB - 1) + TAKEN_STEP)
        bk = fill_v(pe, ("pos",))
        for b in range(TB):
            last = summed(bk[:, b * E:(b + 1) * E], [(ones[:, :], took[:, k, :]) for k in range(b)] + [(tri[:, :], took[:, b, :])])
        last.then_inc(v_filled, 1)
        summed(fill_v(pe, ("cnt",))[:, 0:E], [(ones[:, :], took[:, k, :]) for k in range(TB)]).then_inc(v_filled, 1)
        shared_turned(1)
        shared_up(3)
        pe.wait_ge(oh_made, AHEAD)
        bk = fill_v(pe, ("slots",))
        for e in range(AHEAD):
            last = slot_table(bk[0:CAP, COLS * e:COLS * (e + 1)], e, e)
        last.then_inc(v_filled, 1)
        shared_down(1)
        shared_turned(2)
        shared_turned(3)
        shared_down(2)
        shared_down(3)

        pe.wait_ge(s_emptied, len(FILLS_S))
        pe.wait_ge(v_emptied, len(FILLS_V))

        def tokens(buf, done):
            cols = xg[buf][0:CAP, :].rearrange("p (c k) -> p k c", k=DK)
            transposes(bank[2], [cols[:, k, :] for k in range(4)]).then_inc(done, 1)
            transposes(bank[3], [cols[:, k, :] for k in range(4, 8)]).then_inc(done, 1)

        h_cols = h_sb[0:CAP, :].rearrange("p (c k) -> p k c", k=2)

        def down(s, done):
            for j in range(2):
                summed(bank[5 + j][0:CAP, :], [(hT[:, k, :], Wd[s][:, k, j * 512:(j + 1) * 512]) for k in range(2)]).then_inc(done, 1)

        def tokens_e(e, n):
            pe.wait_ge(gathered[n % 4], (e - n % 4) * 4 + 16)
            if not (isinstance(e, int) and e == 0):
                pe.wait_ge(xgT_s, e)
                pe.wait_ge(xgT_v, e)
            tokens(n % 4, xgT_summed)

        def down_e(e, n, first=False):
            pe.wait_ge(lo_made, e + 1)
            pe.wait_ge(hT_lo_made, e + 1)
            if not first:
                pe.wait_ge(y_s, e)
                pe.wait_ge(y_v, e)
            s = (n + 2) % SLOTS
            for j in range(2):
                cols = slice(j * 512, (j + 1) * 512)
                summed(bank[5 + j][:, :], [pair for k in range(2) for pair in (
                    (hT_hi[:, k, :], wd_hi[n % 2][:, k, cols]), (hT_hi[:, k, :], wd_lo[s][:, k, cols]),
                    (hT_lo[:, k, :], wd_hi[n % 2][:, k, cols]))]).then_inc(down_summed, 1)

        def table_e(e, n, first=False):
            pe.wait_ge(oh_made, e + 1)
            if not first:
                pe.wait_ge(idx_made, (e - AHEAD) * 2)
            slot_table(bank[1][0:CAP, 0:COLS], e, n % AHEAD).then_inc(idx_summed, 1)

        def expert(e, n, first=False, last=False):
            tail = isinstance(e, int) and e >= E - AHEAD
            s = (n + 2) % SLOTS
            pe.wait_ge(w_loaded[s], (e - n % SLOTS) * 12 + 48)
            pe.wait_ge(xgT_s, e + 1)
            pe.wait_ge(xgT_v, e + 1)
            if not first:
                pe.wait_ge(h_made, e)
            gate_up(bank[0][0:CAP, :], xgT[n % 2], Wgu[s]).then_inc(gu_summed, 1)
            if not last:
                tokens_e(e + 1, n + 1)
            if not first:
                down_e(e - 1, n - 1, first=isinstance(e, int) and e == 1)
            if not tail:
                table_e(e + AHEAD, n + AHEAD, first=first)
            pe.wait_ge(h_made, e + 1)
            if not first:
                pe.wait_ge(hT_lo_made, e)
            transposes(bank[4], [h_cols[:, k, :] for k in range(2)]).then_inc(hT_summed, 1)

        tokens_e(0, 0)
        run_experts(pe, expert)
        down_e(E - 1, SLOTS - 1)
        pe.wait_ge(over["shift"], 1)
        most = pe.value_load(cnt_i[0:1, 0:1], min_val=0, max_val=T)
        with pe.If(most > CAP):
            with pe.Fori(1, ROUNDS) as r:
                with pe.Fori(0, E) as e:
                    n = (r - 1) * E + e
                    pe.wait_ge(over["oh"], n + 1)
                    slot_table(bank[1][0:CAP, 0:COLS], e, 0).then_inc(over["idxp"], 1)
                    pe.wait_ge(over["gat"], n * 16 + 16)
                    tokens(0, over["xgTp"])
                    pe.wait_ge(over["xgTs"], n + 1)
                    pe.wait_ge(over["xgTv"], n + 1)
                    pe.wait_ge(over["w"], n * 48 + 48)
                    gate_up(bank[0][0:CAP, :], xgT[0], Wgu[0]).then_inc(over["gu"], 1)
                    pe.wait_ge(over["h"], n + 1)
                    transposes(bank[4], [h_cols[:, k, :] for k in range(2)]).then_inc(over["hTp"], 1)
                    pe.wait_ge(over["hT"], n + 1)
                    down(0, over["dn"])


NAMES = ("x", "mem", "w_in", "q_norm_g", "kv_norm_g", "w_uq", "w_uk", "w_uv", "w_qidx", "rel_bias", "conv_w",
         "w_mem_k", "w_mem_v", "w_out", "ln1_g", "ln1_b", "w_router", "router_bias", "w_e_gate", "w_e_up",
         "w_e_down", "w_s_gate", "w_s_up", "w_s_down", "ln2_g", "ln2_b")


def kernel(**inputs):
    import concourse.bacc as bacc
    from concourse.bass_utils import run_bass_kernel_spmd

    nc = bacc.Bacc("TRN2", target_bir_lowering=False, num_devices=1)
    given = {n: np.ascontiguousarray(inputs[n]) for n in NAMES}
    given["buckets"] = bucket_table()
    arrays = {f"in_{n}": v for n, v in given.items()}
    aps = {n: nc.dram_tensor(f"in_{n}", v.shape, mybir.dt.from_np(v.dtype), kind="ExternalInput").ap() for n, v in given.items()}
    out = nc.dram_tensor("out_0", (1, T, D), F32, kind="ExternalOutput").ap()
    layer_kernel(nc, aps, out)
    r = run_bass_kernel_spmd(nc, [arrays], core_ids=[0])
    return r.results[0]["out_0"]
```
